# Optimizing a Trainium2 kernel written in Bass

```python
import jax, jax.numpy as jnp
from jax import lax
import numpy as np

D_MODEL = 1024
BATCH = 1
SEQ = 512
DEPTH = 2

N_EVEN = (DEPTH + 1) // 2
N_ODD = DEPTH // 2
EPS = 1e-6

D_RNN = D_MODEL // 2
RNN_BLOCKS = 8
RNN_BLOCK_W = D_RNN // RNN_BLOCKS
CONV_W = 4
RGLRU_C = 8.0
FOX_HEADS = 8
FOX_HEAD_DIM = 64
D_FOX = FOX_HEADS * FOX_HEAD_DIM
Q_BLOCK = 128
EVEN_PROJ = 2 * D_RNN + 3 * D_FOX + FOX_HEADS
EVEN_MIX = D_RNN + D_FOX
GLA_HEADS = 4
GLA_DK = D_MODEL // 2
GLA_DV = D_MODEL
GLA_HEAD_DK = GLA_DK // GLA_HEADS
GLA_HEAD_DV = GLA_DV // GLA_HEADS
GATE_RANK = 16
GATE_TAU = 16.0
GLA_CHUNK = 64
ODD_PROJ = 2 * GLA_DK + 2 * GLA_DV + GATE_RANK
N_EXPERTS = 32
N_GROUPS = 4
EXPERTS_PER_GROUP = N_EXPERTS // N_GROUPS
TOP_K = 2
D_EXPERT = D_MODEL // 2
ROUTE_BLOCK = 128

kernel_name = 'hybrid_rglru_fox_gla_grouped_moe_adaln'

F32 = jnp.float32

def rms_norm(x, gain):
    xf = x.astype(F32)
    xf = xf * lax.rsqrt(jnp.mean(xf * xf, axis=-1, keepdims=True) + EPS)
    return (xf * gain.astype(F32)).astype(x.dtype)

def causal_depthwise_conv(x, w, bias):
    ch = x.shape[-1]
    y = lax.conv_general_dilated(x, w[:, None, :], window_strides=(1,), padding=[(CONV_W - 1, 0)],
                                 dimension_numbers=('NWC', 'WIO', 'NWC'), feature_group_count=ch)
    return y + bias

def _linear_combine(left, right):
    a1, b1 = left
    a2, b2 = right
    return a1 * a2, a2 * b1 + b2

def rg_lru(x, r_w, r_b, i_w, i_b, lam):
    b, s, _ = x.shape
    xb = x.reshape(b, s, RNN_BLOCKS, RNN_BLOCK_W)
    r = jax.nn.sigmoid(jnp.einsum('bsnd,nde->bsne', xb, r_w.astype(F32)) + r_b.astype(F32)).reshape(b, s, D_RNN)
    gi = jax.nn.sigmoid(jnp.einsum('bsnd,nde->bsne', xb, i_w.astype(F32)) + i_b.astype(F32)).reshape(b, s, D_RNN)
    log_a = -RGLRU_C * jax.nn.softplus(-lam.astype(F32)) * r
    a = jnp.exp(log_a)
    u = jnp.sqrt(-jnp.expm1(2.0 * log_a)) * (gi * x)
    _, h = lax.associative_scan(_linear_combine, (a, u), axis=1)
    return h

def fox_attention(q, k, v, log_f):
    b, h, s, hd = q.shape
    n_blk = s // Q_BLOCK
    cum = jnp.cumsum(log_f, axis=-1)
    scale = hd ** -0.5
    q_blocks = jnp.moveaxis(q.reshape(b, h, n_blk, Q_BLOCK, hd), 2, 0)
    c_blocks = jnp.moveaxis(cum.reshape(b, h, n_blk, Q_BLOCK), 2, 0)
    k_pos = jnp.arange(s)

    def one_block(args):
        idx, qb, cb = args
        logits = jnp.einsum('bhqd,bhkd->bhqk', qb, k) * scale
        logits = logits + (cb[..., :, None] - cum[..., None, :])
        q_pos = idx * Q_BLOCK + jnp.arange(Q_BLOCK)
        causal = k_pos[None, :] <= q_pos[:, None]
        p = jax.nn.softmax(jnp.where(causal, logits, -jnp.inf), axis=-1)
        return jnp.einsum('bhqk,bhkd->bhqd', p, v)

    out = lax.map(one_block, (jnp.arange(n_blk), q_blocks, c_blocks))
    return jnp.moveaxis(out, 0, 2).reshape(b, h, s, hd)

def gla_chunked(q, k, v, log_g):
    b, h, s, dk = q.shape
    dv = v.shape[-1]
    n = s // GLA_CHUNK
    q = q.reshape(b, h, n, GLA_CHUNK, dk) * (dk ** -0.5)
    k = k.reshape(b, h, n, GLA_CHUNK, dk)
    v = v.reshape(b, h, n, GLA_CHUNK, dv)
    cum = jnp.cumsum(log_g.reshape(b, h, n, GLA_CHUNK, dk), axis=3)
    last = cum[:, :, :, -1:, :]
    q_t = q * jnp.exp(cum)
    k_t = k * jnp.exp(-cum)
    k_end = k * jnp.exp(last - cum)
    mask = jnp.tril(jnp.ones((GLA_CHUNK, GLA_CHUNK), dtype=bool))
    intra = jnp.where(mask, jnp.einsum('bhnqd,bhnkd->bhnqk', q_t, k_t), 0.0)
    o_intra = jnp.einsum('bhnqk,bhnkv->bhnqv', intra, v)
    kv = jnp.einsum('bhnkd,bhnkv->bhndv', k_end, v)
    decay = jnp.exp(last[:, :, :, 0, :])

    def step(state, inp):
        dec, kv_n = inp
        return state * dec[..., None] + kv_n, state

    _, states = lax.scan(step, jnp.zeros((b, h, dk, dv), F32), (jnp.moveaxis(decay, 2, 0), jnp.moveaxis(kv, 2, 0)))
    states = jnp.moveaxis(states, 0, 2)
    o_inter = jnp.einsum('bhnqd,bhndv->bhnqv', q_t, states)
    return (o_intra + o_inter).reshape(b, h, s, dv)

def even_mixer(h, w_in, conv_w, conv_b, r_w, r_b, i_w, i_b, lam, forget_b, q_gain, k_gain, w_out):
    b, s, _ = h.shape
    proj = (h @ w_in).astype(F32)
    splits = np.cumsum([D_RNN, D_RNN, D_FOX, D_FOX, D_FOX]).tolist()
    x_rnn, gate_rnn, q, k, v, f_logit = jnp.split(proj, splits, axis=-1)
    x_rnn = causal_depthwise_conv(x_rnn, conv_w.astype(F32), conv_b.astype(F32))
    y_rnn = rg_lru(x_rnn, r_w, r_b, i_w, i_b, lam) * jax.nn.gelu(gate_rnn)
    def heads(t):
        return t.reshape(b, s, FOX_HEADS, FOX_HEAD_DIM).transpose(0, 2, 1, 3)
    qh = rms_norm(heads(q), q_gain)
    kh = rms_norm(heads(k), k_gain)
    log_f = jax.nn.log_sigmoid(f_logit + forget_b.astype(F32)).transpose(0, 2, 1)
    y_fox = fox_attention(qh, kh, heads(v), log_f).transpose(0, 2, 1, 3).reshape(b, s, D_FOX)
    y = jnp.concatenate([y_rnn, y_fox], axis=-1).astype(h.dtype)
    return y @ w_out

def odd_mixer(h, w_in, gate_w2, gate_b, out_gain, w_out):
    b, s, _ = h.shape
    proj = (h @ w_in).astype(F32)
    splits = np.cumsum([GLA_DK, GLA_DK, GLA_DV, GLA_DV]).tolist()
    q, k, v, r, g_low = jnp.split(proj, splits, axis=-1)
    log_g = jax.nn.log_sigmoid(g_low @ gate_w2.astype(F32) + gate_b.astype(F32)) / GATE_TAU
    def heads(t, d):
        return t.reshape(b, s, GLA_HEADS, d).transpose(0, 2, 1, 3)
    o = gla_chunked(heads(q, GLA_HEAD_DK), heads(k, GLA_HEAD_DK), heads(v, GLA_HEAD_DV), heads(log_g, GLA_HEAD_DK))
    o = rms_norm(o, out_gain).transpose(0, 2, 1, 3).reshape(b, s, GLA_DV)
    y = (o * jax.nn.silu(r)).astype(h.dtype)
    return y @ w_out

def moe_ffn(h, router_w, router_b, w1, w3, w2):
    b, s, d = h.shape
    t = h.reshape(-1, d)
    n_tok = t.shape[0]
    scores = jax.nn.sigmoid(t.astype(F32) @ router_w.astype(F32))
    sel = (scores + router_b.astype(F32)).reshape(n_tok, N_GROUPS, EXPERTS_PER_GROUP)
    group_score = lax.top_k(sel, 2)[0].sum(-1)
    g_idx = jnp.argmax(group_score, axis=-1)
    in_group = jnp.take_along_axis(sel, g_idx[:, None, None], axis=1)[:, 0]
    _, local = lax.top_k(in_group, TOP_K)
    e_idx = g_idx[:, None] * EXPERTS_PER_GROUP + local
    gw = jnp.take_along_axis(scores, e_idx, axis=-1)
    gw = gw / jnp.sum(gw, axis=-1, keepdims=True)
    m = n_tok * TOP_K
    flat_e = e_idx.reshape(-1)
    flat_tok = jnp.repeat(jnp.arange(n_tok), TOP_K)
    flat_w = gw.reshape(-1)
    order = jnp.argsort(flat_e)
    e_sorted = flat_e[order]
    tok_sorted = flat_tok[order]
    counts = jnp.bincount(flat_e, length=N_EXPERTS)
    starts = jnp.cumsum(counts) - counts
    padded = (counts + ROUTE_BLOCK - 1) // ROUTE_BLOCK * ROUTE_BLOCK
    pend = jnp.cumsum(padded)
    pstarts = pend - padded
    dest = pstarts[e_sorted] + (jnp.arange(m) - starts[e_sorted])
    n_blocks = -(-m // ROUTE_BLOCK) + N_EXPERTS
    p_len = n_blocks * ROUTE_BLOCK
    x_pad = jnp.zeros((p_len, d), t.dtype).at[dest].set(t[tok_sorted])
    blk_e = jnp.minimum(jnp.searchsorted(pend, jnp.arange(n_blocks) * ROUTE_BLOCK, side='right'), N_EXPERTS - 1)

    def run_block(args):
        xb, e = args
        hid = jax.nn.silu(xb @ w1[e]) * (xb @ w3[e])
        return hid @ w2[e]

    y_pad = lax.map(run_block, (x_pad.reshape(n_blocks, ROUTE_BLOCK, d), blk_e)).reshape(p_len, d)
    y_sorted = y_pad[dest].astype(F32) * flat_w[order][:, None]
    out = jax.ops.segment_sum(y_sorted, tok_sorted, num_segments=n_tok)
    return out.astype(h.dtype).reshape(b, s, d)

def setup_inputs(seed: int = 0) -> dict:
    key = jax.random.key(seed)
    ks = iter(jax.random.split(key, 64))

    def nrm(shape, scale):
        return jax.random.normal(next(ks), shape, F32) * scale

    u = jax.random.uniform(next(ks), (N_EVEN, D_RNN), F32, 0.9, 0.999)
    a0 = u ** (1.0 / RGLRU_C)
    ev_lam = jnp.log(a0) - jnp.log1p(-a0)
    ev_forget_b = jnp.broadcast_to(jnp.linspace(1.0, 5.0, FOX_HEADS, dtype=F32), (N_EVEN, FOX_HEADS)) + nrm((N_EVEN, FOX_HEADS), 0.1)
    return {
        'x': nrm((BATCH, SEQ, D_MODEL), 1.0),
        'c': nrm((BATCH, D_MODEL), 1.0),
        'router_w': nrm((D_MODEL, N_EXPERTS), D_MODEL ** -0.5),
        'router_b': nrm((N_EXPERTS,), 0.01),
        'ada_w': nrm((DEPTH, D_MODEL, 6 * D_MODEL), 0.5 * D_MODEL ** -0.5),
        'ada_b': nrm((DEPTH, 6 * D_MODEL), 0.02),
        'norm_mix': 1.0 + nrm((DEPTH, D_MODEL), 0.02),
        'norm_ffn': 1.0 + nrm((DEPTH, D_MODEL), 0.02),
        'ev_w_in': nrm((N_EVEN, D_MODEL, EVEN_PROJ), D_MODEL ** -0.5),
        'ev_conv_w': nrm((N_EVEN, CONV_W, D_RNN), 0.5),
        'ev_conv_b': nrm((N_EVEN, D_RNN), 0.02),
        'ev_r_w': nrm((N_EVEN, RNN_BLOCKS, RNN_BLOCK_W, RNN_BLOCK_W), RNN_BLOCK_W ** -0.5),
        'ev_r_b': nrm((N_EVEN, RNN_BLOCKS, RNN_BLOCK_W), 0.02),
        'ev_i_w': nrm((N_EVEN, RNN_BLOCKS, RNN_BLOCK_W, RNN_BLOCK_W), RNN_BLOCK_W ** -0.5),
        'ev_i_b': nrm((N_EVEN, RNN_BLOCKS, RNN_BLOCK_W), 0.02),
        'ev_lam': ev_lam,
        'ev_forget_b': ev_forget_b,
        'ev_q_gain': 1.0 + nrm((N_EVEN, FOX_HEAD_DIM), 0.02),
        'ev_k_gain': 1.0 + nrm((N_EVEN, FOX_HEAD_DIM), 0.02),
        'ev_w_out': nrm((N_EVEN, EVEN_MIX, D_MODEL), EVEN_MIX ** -0.5),
        'od_w_in': nrm((N_ODD, D_MODEL, ODD_PROJ), D_MODEL ** -0.5),
        'od_gate_w2': nrm((N_ODD, GATE_RANK, GLA_DK), GATE_RANK ** -0.5),
        'od_gate_b': nrm((N_ODD, GLA_DK), 0.02),
        'od_out_gain': 1.0 + nrm((N_ODD, GLA_HEAD_DV), 0.02),
        'od_w_out': nrm((N_ODD, GLA_DV, D_MODEL), GLA_DV ** -0.5),
        'moe_w1': nrm((DEPTH, N_EXPERTS, D_MODEL, D_EXPERT), D_MODEL ** -0.5),
        'moe_w3': nrm((DEPTH, N_EXPERTS, D_MODEL, D_EXPERT), D_MODEL ** -0.5),
        'moe_w2': nrm((DEPTH, N_EXPERTS, D_EXPERT, D_MODEL), D_EXPERT ** -0.5),
    }

def reference(x, c, router_w, router_b, ada_w, ada_b, norm_mix, norm_ffn,
              ev_w_in, ev_conv_w, ev_conv_b, ev_r_w, ev_r_b, ev_i_w, ev_i_b, ev_lam, ev_forget_b,
              ev_q_gain, ev_k_gain, ev_w_out,
              od_w_in, od_gate_w2, od_gate_b, od_out_gain, od_w_out,
              moe_w1, moe_w3, moe_w2):
    for layer in range(DEPTH):
        mod = (jax.nn.silu(c) @ ada_w[layer] + ada_b[layer])[:, None, :]
        sh_m, sc_m, g_m, sh_f, sc_f, g_f = jnp.split(mod, 6, axis=-1)
        h = rms_norm(x, norm_mix[layer]) * (1.0 + sc_m) + sh_m
        j = layer // 2
        if layer % 2 == 0:
            y = even_mixer(h, ev_w_in[j], ev_conv_w[j], ev_conv_b[j], ev_r_w[j], ev_r_b[j], ev_i_w[j], ev_i_b[j],
                           ev_lam[j], ev_forget_b[j], ev_q_gain[j], ev_k_gain[j], ev_w_out[j])
        else:
            y = odd_mixer(h, od_w_in[j], od_gate_w2[j], od_gate_b[j], od_out_gain[j], od_w_out[j])
        x = (x + g_m * y).astype(x.dtype)
        h = rms_norm(x, norm_ffn[layer]) * (1.0 + sc_f) + sh_f
        x = (x + g_f * moe_ffn(h, router_w, router_b, moe_w1[layer], moe_w3[layer], moe_w2[layer])).astype(x.dtype)
    return x


_drawn_inputs = setup_inputs


def setup_inputs(seed=0):
    import zlib

    import numpy as np

    out = dict(_drawn_inputs(seed))
    spreads = {}
    factors = {'norm_mix': 3.665,
     'ev_r_b': 8.0,
     'ev_i_b': 8.0,
     'ev_q_gain': 7.592,
     'ev_k_gain': 7.903,
     'od_gate_b': 8.0,
     'od_out_gain': 7.035}
    for name, (base, spread) in spreads.items():
        noise = np.random.default_rng([zlib.crc32(name.encode()), seed]).standard_normal(out[name].shape)
        drawn = base * np.exp(spread * noise) if base else spread * noise
        out[name] = __import__('jax').numpy.asarray(drawn.astype(out[name].dtype))
    for name, factor in factors.items():
        out[name] = (out[name] * factor).astype(out[name].dtype)
    return out
```

```python
import concourse.bass as bass
from concourse import mybir
from contextlib import ExitStack

P = 128
D = 1024
T = 512
TT = T // P
KT = D // P
NC = 512
HEADS = 8
HD = 64
EPS = 1e-6
GH, GDK, GDV = 4, 128, 256
CH = 64
NCH = T // CH
NE = 32
NG, EG = 4, 8
FE = 512
SL = 64
RMAX = T // SL
N_SMALL = 6
SLOTS = 6
PIECE = KT * NC
BIG = 65536.0

RGLRU_C = 8.0
GATE_TAU = 16.0
ADA = [0, 6, 11, 16, 21, 25]
WIN0 = [4, 5, 10, 15, 20]
WOUT0 = [29, 30]
MOE0 = 31
WIN1 = MOE0 + 3 * NE
WOUT1 = WIN1 + 6
MOE1 = WOUT1 + 2


def build_program(nc, A):
    F32, I32, BF16 = mybir.dt.float32, mybir.dt.int32, mybir.dt.bfloat16
    ALU = mybir.AluOpType
    ACT = mybir.ActivationFunctionType
    X_AX = mybir.AxisListType.X
    ds = bass.ds
    vec, act_, pool_, ten = nc.vector, nc.scalar, nc.gpsimd, nc.tensor

    ctx = ExitStack()
    with ctx:
        def sb(name, shape, dt=F32):
            return ctx.enter_context(nc.sbuf_tensor(name, shape, dt))

        def sem(name):
            return ctx.enter_context(nc.semaphore(name))

        mod_d = nc.dram_tensor("mod_d", (2, 12, NC), F32).ap()
        xn_d = [nc.dram_tensor(f"xn_d{l}", (T, D), F32).ap() for l in range(2)]
        y_d = [nc.dram_tensor(f"y_d{l}", (T * 4, NC), F32).ap() for l in range(2)]

        X = sb("X", [P, TT, D])
        hT = sb("hT", [P, KT, T])
        ring = sb("ring", [P, SLOTS, PIECE])
        S = sb("S", [P, 16400])
        ident = sb("ident", [P, P])
        maskneg = sb("maskneg", [P, P])
        blk64 = sb("blk64", [P, P])
        sel = sb("sel", [P, HEADS, P])
        cumx = sb("cumx", [P, T])
        rw_sb = sb("rw_sb", [P, KT, NE])
        gB = sb("gB", [P, D])
        cols = sb("cols", [P, 264])
        rounds_i = sb("rounds_i", [1, 2, NE], I32)

        def carve(base, *shape, parts=P, of=None):
            n = 1
            for s in shape:
                n *= s
            v = (S if of is None else of)[0:parts, base:base + n]
            if len(shape) == 1:
                return v
            names = "abcd"[:len(shape)]
            return v.rearrange(f"p ({' '.join(names)}) -> p {' '.join(names)}",
                               **{k: s for k, s in zip(names[1:], shape[1:])})

        hT_flat = hT[:, :, :].rearrange("p k t -> p (k t)")
        XR_W = T + 4
        xr = carve(0, 4, XR_W)
        gate = carve(4 * XR_W, 4, T)
        qT = carve(4 * XR_W + 2048, 4, T)
        kT = carve(4 * XR_W + 4096, 4, T)
        V0 = 4 * XR_W + 6144
        v_sb = carve(V0, TT, 512)
        wfx = carve(V0, KT, P)
        bd = carve(V0 + 1024, 2, 4, P)
        T0 = V0 + 2048
        xn = carve(T0, TT, D)
        xc = carve(T0, T)
        ri = carve(T0 + 512, 2, T)
        ra = carve(T0 + 1536, T)
        rt = carve(T0 + 2048, T)
        ru = carve(T0 + 2560, T)
        sq = carve(T0 + 3072, 2, T)
        rstd_b = carve(T0 + 4096, 2, T)
        modrow = carve(T0 + 5120, NC)
        biasrow = carve(T0 + 5632, NC)
        prob = carve(T0, 2, T)
        pT = [carve(T0 + 1024, 4, T), carve(2048, 4, T, of=hT_flat)]
        yfT = carve(0, 4, T, of=hT_flat)
        out_tmp = carve(T0 + 4608, NC)

        _c = [0]

        def col(n):
            _c[0] += n
            return cols[:, _c[0] - n:_c[0]]
        cT, cE = col(KT), col(KT)
        ssq, rstd = col(TT), col(TT)
        gain_mf = [col(KT) for _ in range(4)]
        Acol = [col(KT) for _ in range(4)]
        Bcol = [col(KT) for _ in range(4)]
        rbB = col(NE)
        lastc = col(NCH)
        convw, convb, nrb, nib, lamc, gbias = col(16), col(4), col(4), col(4), col(4), col(4)
        qg, kg, fb = col(1), col(1), col(1)
        NPC = 39
        pcols = cols[:, _c[0] - NPC:_c[0]]
        prow = gB[0:NPC, 0:P]
        nsp8, sp_t, lw = col(4), col(4), col(4)
        nmx, rsum, rinv = col(4), col(4), col(4)
        partc, c1p, p4p, idlec = col(1), col(1), col(1), col(1)
        eps_c = col(1)
        keep_screp = sb("screp", [P, KT, 32])
        PS = ctx.enter_context(nc.psum_tensor("PS", [P, 8, 512], F32))

        slot_in = [sem(f"slot_in{i}") for i in range(SLOTS)]
        piece_used = sem("piece_used")
        s_pr = sem("s_pr")
        pr_mm = sem("pr_mm")
        s_prep = sem("s_prep")
        s_c = sem("s_c")
        s_ce = sem("s_ce")
        s_lamx = sem("s_lamx")
        moe_done = sem("moe_done")
        s_silu = sem("s_silu")
        s_kend = sem("s_kend")
        ke_mm = sem("ke_mm")
        oi_mm = sem("oi_mm")
        o_mm = sem("o_mm")
        s_small = sem("s_small")
        s_fx = sem("s_fx")
        s_x = sem("s_x")
        s_const = sem("s_const")
        s_sc = sem("s_sc")
        ada_mm = sem("ada_mm")
        ada_row = sem("ada_row")
        ada_bias = sem("ada_bias")
        ada_st = sem("ada_st")
        s_mod = sem("s_mod")
        s_gB = sem("s_gB")
        s_ab = sem("s_ab")
        s_ss = sem("s_ss")
        s_rstd = sem("s_rstd")
        s_xn = sem("s_xn")
        s_xnst = sem("s_xnst")
        nt_mm = sem("nt_mm")
        nt_a = sem("nt_a")
        nt_v = sem("nt_v")
        job_mm = sem("job_mm")
        job_out = sem("job_out")
        s_sq = sem("s_sq")
        sn_mm = sem("sn_mm")
        s_rsb = sem("s_rsb")
        s_qk = sem("s_qk")
        s_xc = sem("s_xc")
        ri_mm = sem("ri_mm")
        s_ri = sem("s_ri")
        s_rg = sem("s_rg")
        s_at = sem("s_at")
        s_v = sem("s_v")
        s_sqv = sem("s_sqv")
        s_gz = sem("s_gz")
        s_ge = sem("s_ge")
        s_yr = sem("s_yr")
        s_lamE = sem("s_lamE")
        s_lamL = sem("s_lamL")
        s_fl = sem("s_fl")
        s_cum = sem("s_cum")
        sc_mm = sem("sc_mm")
        s_mx = sem("s_mx")
        s_ex = sem("s_ex")
        s_pn = sem("s_pn")
        pt_mm = sem("pt_mm")
        s_pt = sem("s_pt")
        pv_mm = sem("pv_mm")
        s_yf = sem("s_yf")
        wo_mm = sem("wo_mm")
        wo_x = sem("wo_x")
        z_mm = sem("z_mm")
        s_ez = sem("s_ez")
        s_hot = sem("s_hot")
        pos_mm = sem("pos_mm")
        s_tab = sem("s_tab")
        tab_mm = sem("tab_mm")
        s_idx = sem("s_idx")
        g_in = sem("g_in")
        xt_mm = sem("xt_mm")
        s_xt = sem("s_xt")
        h_mm = sem("h_mm")
        s_he = sem("s_he")
        s_hid = sem("s_hid")
        ht_mm = sem("ht_mm")
        s_ht = sem("s_ht")
        y_mm = sem("y_mm")
        s_y = sem("s_y")
        y_st = sem("y_st")
        e_g, e_xt, e_sxt, e_h, e_he, e_hid, e_htm, e_ht, e_ym, e_y, e_st = (
            sem("extra_" + n) for n in ("gather", "xt_mm", "xt", "h_mm", "he", "hid", "ht_mm", "ht", "y_mm", "y", "st"))
        y_in = [sem("y_in0"), sem("y_in1")]
        s_y0 = sem("s_y0")
        s_comb = sem("s_comb")
        s_out = sem("s_out")
        s_small1 = sem("s_small1")
        g1_mm = sem("g1_mm")
        s_g1l = sem("s_g1l")
        s_cm = sem("s_cm")
        s_ec = sem("s_ec")
        it_mm = sem("it_mm")
        s_it = sem("s_it")
        s_ke = sem("s_ke")
        s_st = sem("s_st")
        s_ors = sem("s_ors")
        s_yo = sem("s_yo")
        s_rge = sem("s_rge")
        yt_mm = sem("yt_mm")
        s_yt = sem("s_yt")
        block = ctx.enter_context(nc.Block())

        ada_v = A["ada_w"].rearrange("l (p k) n -> l p k n", k=KT)
        win0_v = A["ev_w_in"].rearrange("a (p k) n -> (a p) k n", k=KT)
        wout0_v = A["ev_w_out"].rearrange("a (k p) n -> (a p) k n", p=P)
        win1_v = A["od_w_in"].rearrange("a (p k) n -> (a p) k n", k=KT)
        wout1_v = A["od_w_out"].rearrange("a (k p) n -> (a p) k n", p=P)
        w1_v = A["moe_w1"].rearrange("l e (p k) f -> (l e) p (k f)", k=KT)
        w3_v = A["moe_w3"].rearrange("l e (p k) f -> (l e) p (k f)", k=KT)
        w2_v = A["moe_w2"].rearrange("l e (h p j) n -> (l e) p h (j n)", h=2, j=2)
        x_v = A["x"].rearrange("b (t p) d -> (b p) t d", p=P)
        out_v = A["out"].rearrange("b (t p) d -> (b p) t d", p=P)
        adab_v = A["ada_b"].rearrange("l (c n) -> (l c) n", n=NC)
        modr = mod_d.rearrange("l c n -> (l c) n")

        def mod_vec(l, which):
            return mod_d[l, 2 * which:2 * which + 2, :]

        def slot_of(piece):
            return piece % SLOTS

        def landed(eng, piece):
            eng.wait_ge(slot_in[piece % SLOTS], 16 * (piece // SLOTS + 1))

        def settle(eng, reg):
            eng.reg_add(reg, reg, 1)

        def piece_ap(piece):
            return ring[:, slot_of(piece), :].rearrange("p (k n) -> p k n", k=KT)

        @block.sync
        def _(sp):
            def load(piece, src):
                if piece >= SLOTS:
                    sp.wait_ge(piece_used, piece - SLOTS + 1)
                dst = piece_ap(piece)
                if len(src.shape) == 2:
                    dst = ring[:, slot_of(piece), :]
                sp.dma_start(dst, src).then_inc(slot_in[slot_of(piece)], 16)

            def stream_experts(layer, first):
                with sp.Fori(0, NE // 2) as it:
                    for u in range(2):
                        e = sp.snap(it * 2 + (layer * NE + u), min_val=0, max_val=2 * NE - 1)
                        for j, w in enumerate((w1_v, w3_v, w2_v)):
                            piece = first + 3 * u + j
                            slot = slot_of(piece)
                            sp.wait_ge(piece_used, it * 6 + (piece - SLOTS + 1))
                            if j < 2:
                                sp.dma_start(ring[:, slot, :], w[ds(e, 1)].rearrange("a p n -> (a p) n"))\
                                    .then_inc(slot_in[slot], 16)
                            else:
                                sp.dma_start(ring[:, slot, :].rearrange("p (h m) -> p h m", h=2),
                                             w[ds(e, 1)].rearrange("a p h m -> (a p) h m"))\
                                    .then_inc(slot_in[slot], 16)

            def load_ada(g):
                for j in range(4):
                    c = (4 * g + j) % 12
                    load(ADA[g] + j, ada_v[g // 3, :, :, c * NC:(c + 1) * NC])

            def load_in0(c):
                load(WIN0[c], win0_v[:, :, c * NC:(c + 1) * NC])
            load_ada(0)
            load_in0(0)
            load_in0(1)
            for c in range(2, 5):
                load_ada(c - 1)
                load_in0(c)
            load_ada(4)
            load_ada(5)
            for c in range(2):
                load(WOUT0[c], wout0_v[:, :, c * NC:(c + 1) * NC])
            stream_experts(0, MOE0)
            for c in range(6):
                load(WIN1 + c, win1_v[:, :, c * NC:(c + 1) * NC])
            for c in range(2):
                load(WOUT1 + c, wout1_v[:, :, c * NC:(c + 1) * NC])
            stream_experts(1, MOE1)

        mxn = carve(0, TT, D)
        xg = carve(4096, 2, D, parts=SL)
        xgT = carve(6144, 2, KT, SL)
        hx = carve(7168, 2 * FE // 2)
        hidb = carve(7680, 2, 256)
        hidT = carve(8192, 2, 2, P)
        ysb = carve(8704, 2, NC)
        RB = 9728
        sc_r = carve(RB, TT, NE)
        sel_r = carve(RB + 128, TT, NE)
        tmp_r = carve(RB + 256, TT, NE)
        O1 = carve(RB + 384, TT, NE)
        O2 = carve(RB + 512, TT, NE)
        wE = carve(RB + 672, NE)
        wG = carve(RB + 704, NG)
        thr = carve(RB + 708, 9)
        top8 = carve(RB + 720, TT * NG, 8)
        gs_r = carve(RB + 848, TT, NG)
        gm_r = carve(RB + 864, TT)
        gv_r = carve(RB + 868, TT, NG)
        wk = col(2 * TT).rearrange("p (k t) -> p k t", k=2)
        assert _c[0] <= 264
        posk = carve(RB + 892, 2, TT)
        ge = carve(RB + 900, 8, 9)
        qm = carve(RB + 972, 2, TT)
        tokv = carve(RB + 980, 2, TT)
        io64 = carve(RB + 988, P)
        Aoh = carve(RB + 1116, 2 * TT, P)
        rvv = carve(RB + 2140, 2 * TT, 8)
        Boh = carve(0, 2, TT, NE * 8)
        hot_b = carve(RB + 3228, TT * NE // 2).bitcast(BF16).rearrange("p (t e) -> p t e", t=TT)
        triS = carve(RB + 3292, P // 2).bitcast(BF16)
        ones_b = carve(RB + 3356, P // 2).bitcast(BF16)
        idx_i = carve(RB + 3420, NE * 8 + 8).bitcast(I32)
        gidx_i = carve(RB + 3684, NE * 8 + 8).bitcast(I32)
        icur = carve(RB + 3948, 2).bitcast(I32)
        gcur = carve(RB + 3950, 2).bitcast(I32)
        ecur = carve(RB + 4304, 2).bitcast(I32)
        tabf = carve(RB + 3952, NE * 8)
        cnt_f = carve(RB + 4208, NE, parts=1)
        rnd_f = carve(RB + 4240, NE, parts=1)
        rc_t = carve(RB + 4272, NE, parts=1)
        yk = [carve(0, 2, D), carve(2048, 2, D)]
        ct = [carve(4096, D), carve(5120, D)]
        assert RB + 4306 <= 16400

        q1 = carve(0, GH, T)
        k1 = carve(2048, GH, T)
        v1 = carve(4096, TT, D)
        r1 = carve(8192, TT, D)
        cum1 = carve(12288, GH, T)
        state = carve(14336, GH, GDV)
        lg_t = carve(14336, 2, T)
        itm = sel[:, 0:4, :]
        ketok = sel[:, 4:8, :]
        ogain = carve(15872, GDV)
        dec1 = carve(16128, GH, NCH)
        tri1 = maskneg
        kend = cum1
        cmask = cumx
        osb = cumx[:, :].rearrange("p (a n) -> p a n", a=2)
        rexp = gB
        yT1 = hT
        wg2 = sel[0:16, 0:4, :].rearrange("p a b -> p (a b)")
        glow = sel[0:16, 4:8, :].rearrange("p a b -> p (a b)")
        gw = blk64[:, :].rearrange("p (k n) -> p k n", k=KT)
        o_ss, o_rs = nmx, rsum

        @block.gpsimd
        def _(pool):
            for m in (ident, maskneg, blk64):
                pool_.memset(m[:, :], 0.0)
            pool_.memset(sel[:, :, :], 0.0)
            pool_.memset(carve(V0, 2048), 0.0)
            pool_.memset(xr[:, :, 0:3], 0.0)
            pool_.memset(gB[0:64, 0:P], 0.0)
            pool_.memset(eps_c, EPS)
            pool.drain()
            pool_.affine_select(out=ident[:, :], in_=ident[:, :], compare_op=ALU.not_equal, fill=1.0, base=0,
                                pattern=[[-1, P]], channel_multiplier=1)
            pool_.affine_select(out=maskneg[:, :], in_=maskneg[:, :], compare_op=ALU.is_ge, fill=-1e30, base=0,
                                pattern=[[-1, P]], channel_multiplier=1)
            pool.drain()
            for o in (0, HD):
                pool_.memset(blk64[o:o + HD, o:o + HD], 1.0)
                pool.drain()
            for base in (0, -64):
                pool_.affine_select(out=sel[:, :, :], in_=sel[:, :, :], compare_op=ALU.not_equal, fill=-1.0,
                                    base=base, pattern=[[-1, HEADS], [0, P]], channel_multiplier=1)
                pool.drain()
            pool_.iota(partc, [[0, 1]], base=0, channel_multiplier=1, allow_small_or_imprecise_dtypes=True)
            pool.drain()
            pool_.tensor_scalar(c1p, partc, 63.5, BIG, ALU.is_gt, ALU.add)
            pool_.tensor_scalar(p4p, partc, 4.0, None, ALU.mult)
            pool.drain()
            pool_.nop().then_inc(s_const, 1)
            row = 0
            for name in ("ev_conv_w", "ev_conv_b", "ev_r_b", "ev_i_b", "ev_lam", "od_gate_b"):
                n = A[name].size() // P
                dims = {2: "a (c p) -> (a c) p", 3: "a j (c p) -> (a j c) p"}
                src = A[name].rearrange(dims[len(A[name].shape)], p=P) if A[name].shape[-1] != HD else \
                    A[name].rearrange("a (c b) e -> (a c) (b e)", b=2)
                pool.dma_start(prow[row:row + n, :], src).then_inc(s_pr, 16)
                row += n
            for o in (0, HD):
                for r, name in enumerate(("ev_q_gain", "ev_k_gain", "ev_forget_b")):
                    pool.dma_start(prow[row + r:row + r + 1, o:o + A[name].size()], A[name]).then_inc(s_pr, 16)
            for o in (0, 64):
                pool.dma_start(wfx[:, :, o:o + HEADS], win0_v[:, :, 2560:2568]).then_inc(s_fx, 16)
            for g, name in enumerate(("ev_r_w", "ev_i_w")):
                wv = A[name].rearrange("a (c b) d e -> b (a d) c e", b=2)
                for b in range(2):
                    pool.dma_start(bd[64 * b:64 * b + 64, g, :, 64 * b:64 * b + 64], wv[b]).then_inc(s_fx, 16)

            def router_consts(layer):
                pool.wait_ge(wo_x, 8 * (layer + 1))
                pool_.iota(wE, [[-1, NE]], base=NE, channel_multiplier=0, allow_small_or_imprecise_dtypes=True)
                pool_.iota(wG, [[-1, NG]], base=NG, channel_multiplier=0, allow_small_or_imprecise_dtypes=True)
                pool_.iota(thr, [[SL, 9]], base=0, channel_multiplier=0, allow_small_or_imprecise_dtypes=True)
                pool_.iota(io64, [[0, 2], [1, SL]], base=0, channel_multiplier=0, allow_small_or_imprecise_dtypes=True)
                pool_.iota(tokv, [[2, 2], [4 * P, TT]], base=-int(BIG), channel_multiplier=4,
                           allow_small_or_imprecise_dtypes=True)
                pool_.memset(ones_b, 1.0)
                pool_.memset(triS, 0.0)
                pool_.memset(xg[:, :, :], 0.0)
                pool.drain()
                pool_.affine_select(out=triS, in_=triS, compare_op=ALU.is_ge, fill=1.0, base=0,
                                    pattern=[[-1, P]], channel_multiplier=1)
                pool.drain()
                pool_.nop().then_inc(s_const, 1)

            def tick():
                pool_.tensor_tensor(idlec, partc, partc, ALU.add)
                pool.drain()

            def table_column(dst, table, parts, column):
                pool_.tensor_copy(dst[0:parts, 0:1], table[0:parts, ds(column, 1)])
                pool.drain()

            def gather(layer, par, done, index=gcur):
                pool_.indirect_dma_start(xg[:, par, :], None, xn_d[layer],
                                         bass.IndirectOffsetOnAxis(index[0:SL, 0:1], 0),
                                         bounds_check=T - 1, oob_is_err=False).then_inc(done, 16)

            def scatter(layer, par, done):
                pool_.indirect_dma_start(y_d[layer], bass.IndirectOffsetOnAxis(icur[:, 0:1], 0),
                                         ysb[:, par, :], None,
                                         bounds_check=4 * T - 1, oob_is_err=False).then_inc(done, 16)

            extra = pool.alloc_register("pool_extra")
            pool.reg_mov(extra, 0)

            def moe(layer):
                b = layer * NE
                bg = layer * (NE + 1)
                pool.wait_ge(s_idx, layer + 1)
                table_column(gcur, gidx_i, SL, 0)
                gather(layer, 0, g_in)
                with pool.Fori(0, NE // 2) as it:
                    for u in range(2):
                        e = pool.snap(it * 2 + u, min_val=0, max_val=NE - 1)
                        rounds = pool.value_load(rounds_i[0:1, layer, ds(e, 1)], min_val=1, max_val=RMAX)
                        pool.wait_ge(g_in, it * 32 + 16 * (bg + u + 1))
                        tick()
                        table_column(gcur, gidx_i, SL, e * 8 + 8)
                        gather(layer, 1 - u, g_in)
                        table_column(icur, idx_i, P, e * 8)
                        pool.wait_ge(s_y, it * 2 + (b + u + 1))
                        tick()
                        scatter(layer, u, y_st)
                        pool.wait_ge(y_st, it * 32 + 16 * (b + u + 1))
                        tick()
                        with pool.If(rounds > 1):
                            with pool.Fori(1, rounds) as r:
                                pool.reg_add(extra, extra, 1)
                                n = pool.snap(extra, min_val=1, max_val=2 * NE * RMAX)
                                c = pool.snap(e * 8 + r, min_val=0, max_val=NE * 8 - 1)
                                table_column(ecur, gidx_i, SL, c)
                                gather(layer, u, e_g, ecur)
                                table_column(icur, idx_i, P, c)
                                pool.wait_ge(e_y, n)
                                tick()
                                scatter(layer, u, e_st)
                                pool.wait_ge(e_st, n * 16)
                                tick()
                            pool.drain()
                        pool.drain()
                pool.wait_ge(g_in, 16 * (bg + NE + 1))
                pool.drain()
                pool_.nop().then_inc(moe_done, 1)

            def load_rows(layer):
                yv = y_d[layer].rearrange("(t p c) n -> t p (c n)", p=P, c=4)
                for t in range(TT):
                    n = layer * TT + t
                    if t >= 2:
                        pool.wait_ge(s_comb, n - 1)
                    pool.dma_start(yk[t % 2].rearrange("p a n -> p (a n)"), yv[t]).then_inc(y_in[t % 2], 16)

            def adaln_out(g):
                for j in range(4):
                    pool.dma_start(biasrow[32 * j:32 * j + 32, :],
                                   adab_v[4 * g + j:4 * g + j + 1, :].partition_broadcast(32)
                                   .rearrange("p a n -> p (a n)")).then_inc(ada_bias, 16)
                pool.wait_ge(ada_bias, 64 * (g + 1))
                pool.wait_ge(ada_row, g + 1)
                pool_.tensor_tensor(modrow, modrow, biasrow, ALU.add)
                pool.drain()
                pool.dma_start(modr[4 * g:4 * g + 4, :], modrow[0:P:32, :]).then_inc(ada_st, 16)
                pool.wait_ge(ada_st, 16 * (g + 1))

            def load_mod(n):
                layer, ffn = n // 2, n % 2
                for dst, which in ((Bcol[n], 3 * ffn), (Acol[n], 3 * ffn + 1)):
                    pool.dma_start(dst, mod_vec(layer, which).rearrange("c (q k) -> (c q) k", k=KT))\
                        .then_inc(s_mod, 16)

            def load_gate(layer, ffn):
                src = mod_vec(layer, 3 * ffn + 2).rearrange("c n -> (c n)")
                pool.dma_start(gB[:, :], src.partition_broadcast(P)).then_inc(s_gB, 16)

            def store_xn(layer):
                for t in range(TT):
                    pool.wait_ge(s_xn, 4 * (2 * layer + 1) + t + 1)
                    pool.dma_start(xn_d[layer][t * P:(t + 1) * P, :], mxn[:, t, :]).then_inc(s_xnst, 16)
                pool.wait_ge(s_xnst, 64 * (layer + 1))

            def qk_scale(m):
                pool.wait_ge(s_rsb, m + 1)
                dst = (qT if m < 4 else kT)[:, m % 4, :]
                pool_.tensor_tensor(dst, dst, rstd_b[:, m % 2, :], ALU.mult).then_inc(s_qk, 1)

            adaln_out(0)
            load_mod(0)
            adaln_out(1)
            load_gate(0, 0)
            for m in range(3):
                qk_scale(m)
            adaln_out(2)
            load_mod(1)
            for m in range(3, 7):
                qk_scale(m)
            adaln_out(3)
            load_mod(2)
            qk_scale(7)
            adaln_out(4)
            adaln_out(5)
            load_mod(3)
            router_consts(0)
            load_gate(0, 1)
            pool.dma_start(gw, win1_v[:, :, 3072:3088]).then_inc(s_small1, 16)
            pool.dma_start(wg2, A["od_gate_w2"].rearrange("a r n -> (a r) n")).then_inc(s_small1, 16)
            pool_.memset(cmask[:, :], 1.0)
            pool.drain()
            pool_.memset(cmask[:, :].rearrange("p (n c) -> p n c", c=CH)[:, :, 0:1], 0.0)
            pool_.memset(tri1[:, :], 1.0)
            pool.drain()
            pool_.affine_select(out=tri1[:, :], in_=tri1[:, :], compare_op=ALU.is_ge, fill=0.0, base=0,
                                pattern=[[1, P]], channel_multiplier=-1)
            pool.drain()
            pool_.memset(tri1[0:CH, CH:P], 0.0)
            pool.drain()
            pool_.nop().then_inc(s_const, 1)
            store_xn(0)
            moe(0)
            load_rows(0)
            pool.wait_ge(s_comb, TT)
            pool.dma_start(ogain, A["od_out_gain"].rearrange("a n -> (a n)").partition_broadcast(P))\
                .then_inc(s_small1, 16)
            pool.wait_ge(s_silu, TT)
            load_gate(1, 0)
            router_consts(1)
            load_gate(1, 1)
            store_xn(1)
            moe(1)
            load_rows(1)

        def q_job(m):
            return ("job", 9 + m)
        ORDER0 = ([("job", 0), ("lam", 0)] + [("job", n) for n in (1, 2, 3, 4, 5, 6)] + [("ri", 0)]
                  + [("job", 7), ("job", 8), ("ri", 1), ("ada", 1)]
                  + [q_job(0), q_job(1), ("sn", 0), ("ri", 2), q_job(2), ("sn", 1), q_job(3), ("sn", 2), ("ri", 3)]
                  + [("ada", 2)]
                  + [q_job(4), ("sn", 3), q_job(5), ("sn", 4), q_job(6), ("sn", 5), q_job(7), ("sn", 6)]
                  + [("ada", 3)]
                  + [("job", 17), ("sn", 7)] + [("job", n) for n in (18, 19, 20)] + [("ada", 4)])
        JOBS0 = 21
        ORDER1 = ([("job", 0)] + [("job", 1), ("g1", 0)] + [("job", 2), ("job", 3), ("job", 4)]
                  + [("job", 5), ("g1", 1), ("job", 6), ("g1", 2), ("job", 7), ("g1", 3), ("job", 8)]
                  + [("job", n) for n in range(9, 25)])
        JOBS1 = 25

        def job_bank(n):
            return n % 4

        @block.scalar
        def _(act):
            act.dma_start(cT, A["c"].rearrange("a (p k) -> (a p) k", k=KT)).then_inc(s_c, 16)
            for t in range(TT):
                act.dma_start(X[:, t, :], x_v[:, t, :]).then_inc(s_x, 16)
            small = [(gain_mf[2 * l + f], A[("norm_mix", "norm_ffn")[f]][l:l + 1, :].rearrange("a (p k) -> (a p) k", k=KT))
                     for l in range(2) for f in range(2)]
            small += [(rw_sb[:, :, :], A["router_w"].rearrange("(p k) e -> p k e", k=KT)),
                      (rbB, A["router_b"].partition_broadcast(P))]
            for dst, src in small:
                act.dma_start(dst, src).then_inc(s_small, 16)
            assert len(small) == N_SMALL

            act.wait_ge(s_c, 16)
            act_.activation(cE, cT, ACT.Exp, scale=-1.0).then_inc(s_ce, 1)
            act.wait_ge(s_const, 1)

            def adaln_move(g):
                act.wait_ge(ada_mm, g + 1)
                if g:
                    act.wait_ge(ada_st, 16 * g)
                act_.activation(modrow, PS[:, 4, :], ACT.Copy).then_inc(ada_row, 1)

            def rms_from(dst, src, n):
                act_.activation(dst, src, ACT.Ln, scale=1.0 / n, bias=eps_c)
                act.drain()
                return act_.activation(dst, dst, ACT.Exp, scale=-0.5)

            def norm(n, xbuf):
                layer, ffn = n // 2, n % 2
                for t in range(TT):
                    if n == 0:
                        act.wait_ge(s_x, 16 * TT)
                    elif ffn:
                        act.wait_ge(wo_x, 8 * layer + 8)
                    else:
                        act.wait_ge(s_comb, t + 1)
                    act_.activation(xbuf[:, t, :], X[:, t, :], ACT.Square, accum_out=ssq[:, t:t + 1])
                act.drain()
                rms_from(rstd, ssq, D).then_inc(s_rstd, 1)
                act.wait_ge(s_ab, n + 1)
                for kt in range(0, KT, 2):
                    act.wait_ge(nt_mm, 8 * n + kt + 1)
                    act_.activation(hT[:, kt, :], PS[:, 6 + kt % 2, :], ACT.Identity,
                                    scale=Acol[n][:, kt:kt + 1], bias=Bcol[n][:, kt:kt + 1]).then_inc(nt_a, 1)

            def job0(n):
                act.wait_ge(job_mm, n + 1)
                src = PS[:, job_bank(n), :]
                if n == 0:
                    act_.activation(cumx[:, :], src, ACT.Identity, bias=fb).then_inc(job_out, 1)
                    act.drain()
                    act_.activation(rt, cumx[:, :], ACT.Abs)
                    act.drain()
                    act_.activation(rt, rt, ACT.Exp, scale=-1.0)
                    act.drain()
                    act_.activation(rt, rt, ACT.Ln, bias=1.0).then_inc(s_fl, 1)
                elif n < 5:
                    act_.activation(xr[:, n - 1, 3:3 + T], src, ACT.Copy).then_inc(job_out, 1)
                elif n < 9:
                    act_.activation(gate[:, n - 5, :], src, ACT.Copy).then_inc(job_out, 1)
                elif n < 17:
                    m = n - 9
                    if m >= 2:
                        act.wait_ge(sn_mm, m - 1)
                    act_.activation(sq[:, m % 2, :], src, ACT.Square).then_inc(s_sq, 1)
                    dst, gain = (qT, qg) if m < 4 else (kT, kg)
                    act_.activation(dst[:, m % 4, :], src, ACT.Identity, scale=gain).then_inc(job_out, 1)
                else:
                    if n == 17:
                        act.wait_ge(ri_mm, 4)
                    act_.activation(v_sb[:, n - 17, :], src, ACT.Copy).then_inc(job_out, 1)

            def head_norm(m):
                act.wait_ge(sn_mm, m + 1)
                if m >= 2:
                    act.wait_ge(s_qk, m - 1)
                rms_from(rstd_b[:, m % 2, :], PS[:, 5, :], HD).then_inc(s_rsb, 1)

            def rnn_gates(c):
                act.wait_ge(ri_mm, c + 1)
                if c:
                    act.wait_ge(s_yr, c)
                act_.activation(ri[:, 0, :], PS[:, 6, :], ACT.Exp, scale=-1.0, bias=nrb[:, c:c + 1])
                act_.activation(ri[:, 1, :], PS[:, 7, :], ACT.Exp, scale=-1.0, bias=nib[:, c:c + 1]).then_inc(s_ri, 1)
                act.wait_ge(s_gz, c + 1)
                act_.activation(ru, ru, ACT.Exp, scale=-1.5957691216057308).then_inc(s_ge, 1)
                act.wait_ge(s_rg, c + 1)
                act_.activation(ra, ri[:, 0, :], ACT.Exp, scale=nsp8[:, c:c + 1])
                act_.activation(rt, ri[:, 0, :], ACT.Tanh, scale=nsp8[:, c:c + 1]).then_inc(s_at, 1)
                act.wait_ge(s_v, c + 1)
                act_.activation(rt, rt, ACT.Sqrt).then_inc(s_sqv, 1)

            def lam_stage():
                act.wait_ge(s_lamE, 1)
                act_.activation(sp_t, sp_t, ACT.Exp, scale=-1.0).then_inc(s_lamx, 1)
                act.wait_ge(s_lamL, 1)
                act_.activation(nsp8, lw, ACT.Ln).then_inc(s_lamx, 1)

            adaln_move(0)
            norm(0, xn)
            act.wait_ge(s_prep, 1)
            for kind, i in ORDER0:
                if kind == "job":
                    job0(i)
                elif kind == "lam":
                    lam_stage()
                elif kind == "sn":
                    head_norm(i)
                elif kind == "ri":
                    rnn_gates(i)
                else:
                    adaln_move(i)

            def exps(n):
                h, t = divmod(n, TT)
                N = P * (t + 1)
                act.wait_ge(s_mx, n + 1)
                if n >= 2:
                    act.wait_ge(pt_mm, n - 1)
                act_.activation(prob[:, n % 2, 0:N], PS[:, n % 4, 0:N], ACT.Exp, bias=nmx[:, n % 4:n % 4 + 1],
                                accum_out=rsum[:, n % 4:n % 4 + 1]).then_inc(s_ex, 1)

            def move_pt(n):
                h, t = divmod(n, TT)
                act.wait_ge(pt_mm, n + 1)
                if h >= 2:
                    act.wait_ge(pv_mm, h // 2)
                act_.activation(pT[h % 2][:, 0:t + 1, t * P:(t + 1) * P],
                                PS[:, 4 + n % 2, 0:P * (t + 1)].rearrange("p (k q) -> p k q", q=P),
                                ACT.Copy).then_inc(s_pt, 1)
                if n % 8 == 7:
                    act.wait_ge(pv_mm, h // 2 + 1)
                    act_.activation(yfT[:, h // 2, :], PS[:, 6 + h // 2 % 2, :], ACT.Copy).then_inc(s_yf, 1)

            exps(0)
            for n in range(HEADS * TT):
                if n + 1 < HEADS * TT:
                    exps(n + 1)
                move_pt(n)
            adaln_move(5)
            norm(1, mxn)

            def moe(layer):
                b = layer * NE
                act.wait_ge(z_mm, layer + 1)
                act_.activation(sc_r, PS[:, 7, 0:TT * NE].rearrange("p (t e) -> p t e", t=TT), ACT.Exp,
                                scale=-1.0).then_inc(s_ez, 1)
                act.wait_ge(s_idx, layer + 1)

                def expert_round(par, hidden, expo, transposed, moved, made, out):
                    act.wait_ge(*hidden)
                    act_.activation(hx[:, 0:256], PS[:, 2, 0:256], ACT.Exp, scale=-1.0).then_inc(expo, 1)
                    act.wait_ge(*transposed)
                    act_.activation(hidT[:, par, :, :], PS[:, 4, 0:256].rearrange("p (j s) -> p j s", j=2),
                                    ACT.Copy).then_inc(moved, 1)
                    act.wait_ge(*made)
                    act_.activation(ysb[:, par, :], PS[:, 5 + par, :], ACT.Copy).then_inc(out, 1)

                with act.Fori(0, NE // 2) as it:
                    for u in range(2):
                        e = act.snap(it * 2 + u, min_val=0, max_val=NE - 1)
                        rounds = act.value_load(rounds_i[0:1, layer, ds(e, 1)], min_val=1, max_val=RMAX)
                        k = act.snap(it * 2 + (b + u + 1), min_val=1, max_val=2 * NE)
                        expert_round(u, (h_mm, k), s_he, (ht_mm, k), s_ht, (y_mm, k), s_y)
                        with act.If(rounds > 1):
                            with act.Fori(1, rounds) as r:
                                act.reg_add(extra_a, extra_a, 1)
                                n = act.snap(extra_a, min_val=1, max_val=2 * NE * RMAX)
                                expert_round(u, (e_h, n), e_he, (e_htm, n), e_ht, (e_ym, n), e_y)
                                act.wait_ge(e_st, n * 16)
                                settle(act, idle)
                            act.drain()
                        act.drain()

            def combine(layer):
                for t in range(TT):
                    n = layer * TT + t
                    act.wait_ge(y_in[t % 2], 16 * (2 * layer + t // 2 + 1))
                    if t >= 2:
                        act.wait_ge(s_comb, n - 1)
                    act_.activation(ct[t % 2], yk[t % 2][:, 0, :], ACT.Identity,
                                    scale=wk[:, 0, t:t + 1]).then_inc(s_y0, 1)

            extra_a = act.alloc_register("act_extra")
            act.reg_mov(extra_a, 0)
            idle = act.alloc_register("act_idle")
            act.reg_mov(idle, 0)
            moe(0)
            combine(0)
            act.drain()

            norm(2, xn)

            def job1(n):
                act.wait_ge(job_mm, JOBS0 + n + 1)
                src = PS[:, job_bank(n), :]
                if n == 0:
                    act_.activation(glow, src[0:16, :], ACT.Copy).then_inc(job_out, 1)
                elif n < 9:
                    dst = q1 if n < 5 else k1
                    act_.activation(dst[:, (n - 1) % 4, :], src, ACT.Copy).then_inc(job_out, 1)
                elif n < 17:
                    half, t = divmod(n - 9, TT)
                    act_.activation(v1[:, t, half * 512:half * 512 + 512], src, ACT.Copy).then_inc(job_out, 1)
                else:
                    half, t = divmod(n - 17, TT)
                    act_.activation(r1[:, t, half * 512:half * 512 + 512], src, ACT.Copy).then_inc(job_out, 1)

            def gates1(h):
                act.wait_ge(g1_mm, h + 1)
                if h:
                    act.wait_ge(s_kend, h)
                act_.activation(lg_t[:, 0, :], PS[:, 4 + h % 2, :], ACT.Identity, bias=gbias[:, h:h + 1])
                act.drain()
                act_.activation(lg_t[:, 1, :], lg_t[:, 0, :], ACT.Abs)
                act.drain()
                act_.activation(lg_t[:, 1, :], lg_t[:, 1, :], ACT.Exp, scale=-1.0)
                act.drain()
                act_.activation(lg_t[:, 1, :], lg_t[:, 1, :], ACT.Ln, bias=1.0).then_inc(s_g1l, 1)
                act.wait_ge(s_cm, h + 1)
                ends = cum1[:, h, :].rearrange("p (n c) -> p n c", c=CH)[:, :, CH - 1]
                act_.activation(lastc, ends, ACT.Copy)
                act_.activation(dec1[:, h, :], ends, ACT.Exp)
                act_.activation(lg_t[:, 0, :], cum1[:, h, :], ACT.Exp)
                act_.activation(lg_t[:, 1, :], cum1[:, h, :], ACT.Exp, scale=-1.0)
                act.drain()
                for n in range(NCH):
                    part = cum1[:, h, n * CH:(n + 1) * CH]
                    last = act_.activation(part, part, ACT.Exp, scale=-1.0, bias=lastc[:, n:n + 1])
                last.then_inc(s_ec, 1)

            for kind, i in ORDER1:
                if kind == "job":
                    job1(i)
                    if 5 <= i < 9:
                        gates1(i - 5)

            def gla_tile(t):
                act.drain()
                if t:
                    act.wait_ge(s_silu, t)
                act_.activation(rexp[:, :], r1[:, t, :], ACT.Exp, scale=-1.0).then_inc(s_rge, 1)
                act.wait_ge(ke_mm, t + 1)
                act_.activation(ketok, PS[:, 1, :].rearrange("p (h n) -> p h n", h=GH), ACT.Copy).then_inc(s_ke, 1)
                for h in range(GH):
                    i = GH * t + h
                    act.wait_ge(o_mm, i + 1)
                    act_.activation(PS[:, 2 + h, 256:512], PS[:, 2 + h, 0:256], ACT.Square,
                                    accum_out=o_ss[:, h:h + 1])
                act.drain()
                rms_from(o_rs, o_ss, GDV).then_inc(s_ors, 1)
                for half in range(2):
                    act.wait_ge(yt_mm, 2 * t + half + 1)
                    act_.activation(yT1[:, 4 * half:4 * half + 4, t * P:(t + 1) * P],
                                    PS[:, half, :].rearrange("p (k q) -> p k q", q=P), ACT.Copy).then_inc(s_yt, 1)

            for t in range(TT):
                gla_tile(t)
            norm(3, mxn)
            moe(1)
            combine(1)
            for t in range(TT):
                act.wait_ge(s_comb, TT + t + 1)
                act.dma_start(out_v[:, t, :], X[:, t, :]).then_inc(s_out, 16)
            act.wait_ge(s_out, 16 * TT)

        @block.vector
        def _(dve):
            dve.wait_ge(s_ce, 1)
            vec.tensor_scalar(cE, cE, 1.0, None, ALU.add)
            dve.drain()
            vec.reciprocal(cE, cE)
            dve.drain()
            vec.tensor_tensor(cE, cE, cT, ALU.mult)
            dve.drain()
            vec.tensor_copy(keep_screp[:, :, :], cE.unsqueeze(2).broadcast_to([P, KT, 32])).then_inc(s_sc, 1)
            dve.wait_ge(s_small, 16 * N_SMALL)
            dve.wait_ge(pr_mm, 1)
            vec.tensor_copy(pcols, PS[:, 5, 0:NPC])
            dve.drain()
            vec.tensor_scalar(nrb, nrb, -1.0, None, ALU.mult)
            vec.tensor_scalar(nib, nib, -1.0, None, ALU.mult)
            vec.scalar_tensor_tensor(out=sp_t, in0=lamc, scalar=-1.0, in1=lamc, op0=ALU.mult, op1=ALU.max)
            vec.tensor_scalar(qg, qg, HD ** -0.5, None, ALU.mult).then_inc(s_prep, 1)
            dve.drain()

            def columns(n):
                dve.wait_ge(s_mod, 32 * (n + 1))
                vec.scalar_tensor_tensor(out=Acol[n], in0=Acol[n], scalar=1.0, in1=gain_mf[n],
                                         op0=ALU.add, op1=ALU.mult).then_inc(s_ab, 1)

            def norm(n, xbuf):
                dve.wait_ge(s_rstd, n + 1)
                for t in range(TT):
                    vec.tensor_scalar(xbuf[:, t, :], X[:, t, :], rstd[:, t:t + 1], None, ALU.mult).then_inc(s_xn, 1)
                columns(n)
                dve.drain()
                for kt in range(1, KT, 2):
                    dve.wait_ge(nt_mm, 8 * n + kt + 1)
                    vec.tensor_scalar(hT[:, kt, :], PS[:, 6 + kt % 2, :], Acol[n][:, kt:kt + 1],
                                      Bcol[n][:, kt:kt + 1], ALU.mult, ALU.add).then_inc(nt_v, 1)

            def lam_stage():
                dve.nop().then_inc(s_lamE, 1)
                dve.wait_ge(s_lamx, 1)
                vec.tensor_scalar(lw, sp_t, 1.0, None, ALU.add).then_inc(s_lamL, 1)
                dve.drain()
                vec.scalar_tensor_tensor(out=sp_t, in0=lw, scalar=-1.0, in1=sp_t, op0=ALU.add, op1=ALU.subtract)
                dve.wait_ge(s_lamx, 2)
                dve.drain()
                vec.reciprocal(lw, lw)
                dve.drain()
                vec.tensor_tensor(sp_t, sp_t, lw, ALU.mult)
                dve.drain()
                vec.tensor_tensor(nsp8, nsp8, sp_t, ALU.subtract)
                dve.drain()
                vec.tensor_scalar(sp_t, lamc, -1.0, 0.0, ALU.mult, ALU.max)
                dve.drain()
                vec.tensor_tensor(nsp8, nsp8, sp_t, ALU.add)
                dve.drain()
                vec.tensor_scalar(nsp8, nsp8, -RGLRU_C, None, ALU.mult)
                dve.drain()

            def one_over_one_plus(x):
                vec.tensor_scalar(x, x, 1.0, None, ALU.add)
                dve.drain()
                return vec.reciprocal(x, x)

            def rnn(c):
                dve.wait_ge(job_out, c + 2)
                vec.tensor_scalar(xc, xr[:, c, 3:3 + T], convw[:, 12 + c:13 + c], convb[:, c:c + 1],
                                  ALU.mult, ALU.add)
                dve.drain()
                for j in range(3):
                    ins = vec.scalar_tensor_tensor(out=xc, in0=xr[:, c, j:j + T], scalar=convw[:, 4 * j + c:4 * j + c + 1],
                                                   in1=xc, op0=ALU.mult, op1=ALU.add)
                    if j == 2:
                        ins.then_inc(s_xc, 1)
                    dve.drain()
                dve.wait_ge(job_out, c + 6)
                vec.tensor_tensor(ru, gate[:, c, :], gate[:, c, :], ALU.mult)
                dve.drain()
                vec.tensor_scalar(ru, ru, 0.044715, 1.0, ALU.mult, ALU.add)
                dve.drain()
                vec.tensor_tensor(ru, ru, gate[:, c, :], ALU.mult)
                dve.drain()
                vec.tensor_scalar(ru, ru, -54.0, None, ALU.max).then_inc(s_gz, 1)
                dve.wait_ge(s_ri, c + 1)
                one_over_one_plus(ri[:, :, :]).then_inc(s_rg, 1)
                dve.wait_ge(s_ge, c + 1)
                one_over_one_plus(ru)
                dve.drain()
                vec.tensor_tensor(gate[:, c, :], gate[:, c, :], ru, ALU.mult)
                vec.tensor_tensor(xc, xc, ri[:, 1, :], ALU.mult)
                dve.drain()
                dve.wait_ge(s_at, c + 1)
                vec.tensor_scalar(ru, rt, -1.0, 1.0, ALU.mult, ALU.add)
                dve.drain()
                vec.reciprocal(ru, ru)
                dve.drain()
                vec.scalar_tensor_tensor(out=rt, in0=rt, scalar=-2.0, in1=ru, op0=ALU.mult, op1=ALU.mult)\
                    .then_inc(s_v, 1)
                dve.wait_ge(s_sqv, c + 1)
                vec.tensor_tensor(xc, xc, rt, ALU.mult)
                dve.drain()
                vec.tensor_tensor_scan(rt, ra, xc, 0.0, ALU.mult, ALU.add)
                dve.drain()
                vec.tensor_tensor(xr[:, c, 3:3 + T], rt, gate[:, c, :], ALU.mult).then_inc(s_yr, 1)
                dve.drain()

            dve.wait_ge(s_x, 16 * TT)
            norm(0, xn)
            lam_stage()
            dve.wait_ge(s_fl, 1)
            vec.scalar_tensor_tensor(out=cumx[:, :], in0=cumx[:, :], scalar=0.0, in1=rt, op0=ALU.min, op1=ALU.subtract)
            vec.memset(ru, 1.0)
            dve.drain()
            vec.tensor_tensor_scan(cumx[:, :], ru, cumx[:, :], 0.0, ALU.mult, ALU.add).then_inc(s_cum, 1)
            dve.drain()
            for c in range(4):
                rnn(c)

            def row_max(n):
                h, t = divmod(n, TT)
                dve.wait_ge(sc_mm, n + 1)
                diag = PS[:, n % 4, t * P:(t + 1) * P]
                vec.tensor_tensor(diag, diag, maskneg[:, :], ALU.add)
                dve.drain()
                vec.tensor_reduce(nmx[:, n % 4:n % 4 + 1], PS[:, n % 4, 0:P * (t + 1)], X_AX, ALU.max,
                                  negate=True).then_inc(s_mx, 1)

            row_max(0)
            for n in range(HEADS * TT):
                if n + 1 < HEADS * TT:
                    row_max(n + 1)
                N = P * (n % TT + 1)
                dve.wait_ge(s_ex, n + 1)
                vec.reciprocal(rinv[:, n % 4:n % 4 + 1], rsum[:, n % 4:n % 4 + 1])
                dve.drain()
                vec.tensor_scalar(prob[:, n % 2, 0:N], prob[:, n % 2, 0:N], rinv[:, n % 4:n % 4 + 1], None,
                                  ALU.mult).then_inc(s_pn, 1)

            def add_output(layer, bank0):
                dve.wait_ge(s_gB, 16 * (2 * layer + 1))
                for o in range(8):
                    half, t = divmod(o, TT)
                    cs = slice(half * NC, (half + 1) * NC)
                    dve.wait_ge(wo_mm, 8 * layer + o + 1)
                    vec.tensor_tensor(out_tmp, PS[:, bank0 + o % 4, :], gB[:, cs], ALU.mult)
                    dve.drain()
                    vec.tensor_tensor(X[:, t, cs], X[:, t, cs], out_tmp, ALU.add).then_inc(wo_x, 1)
                    dve.drain()

            def bc(ap, *shape):
                return ap.broadcast_to([P, *shape])

            def pick(O):
                vec.tensor_reduce(gm_r, sel_r, X_AX, ALU.max)
                dve.drain()
                vec.tensor_tensor(O, sel_r, bc(gm_r.unsqueeze(2), TT, NE), ALU.is_ge)
                dve.drain()
                vec.tensor_tensor(O, O, bc(wE.unsqueeze(1), TT, NE), ALU.mult)
                dve.drain()
                vec.tensor_reduce(gm_r, O, X_AX, ALU.max)
                dve.drain()
                vec.tensor_tensor(O, O, bc(gm_r.unsqueeze(2), TT, NE), ALU.is_equal)
                dve.drain()

            def router(layer):
                dve.wait_ge(s_const, 3 if layer == 0 else 4)
                dve.wait_ge(s_ez, layer + 1)
                one_over_one_plus(sc_r)
                dve.drain()
                vec.tensor_tensor(sel_r, sc_r, bc(rbB.unsqueeze(1), TT, NE), ALU.add)
                dve.drain()
                for i in range(TT * NG):
                    t, g = divmod(i, NG)
                    vec.max(top8[:, i, :], sel_r[:, t, g * EG:(g + 1) * EG])
                dve.drain()
                vec.tensor_tensor(gs_r.rearrange("p t g -> p (t g)"), top8[:, :, 0], top8[:, :, 1], ALU.add)
                dve.drain()
                vec.tensor_reduce(gm_r, gs_r, X_AX, ALU.max)
                dve.drain()
                vec.tensor_tensor(gv_r, gs_r, bc(gm_r.unsqueeze(2), TT, NG), ALU.is_ge)
                dve.drain()
                vec.tensor_tensor(gv_r, gv_r, bc(wG.unsqueeze(1), TT, NG), ALU.mult)
                dve.drain()
                vec.tensor_reduce(gm_r, gv_r, X_AX, ALU.max)
                dve.drain()
                vec.tensor_tensor(gv_r, gv_r, bc(gm_r.unsqueeze(2), TT, NG), ALU.is_equal)
                dve.drain()
                flat = sel_r.rearrange("p t (g x) -> p (t g) x", g=NG)
                gvf = gv_r.rearrange("p t g -> p (t g)")
                vec.tensor_scalar(gs_r, gv_r, 1e30, -1e30, ALU.mult, ALU.add)
                vec.tensor_tensor(flat, flat, bc(gvf.unsqueeze(2), TT * NG, EG), ALU.mult)
                dve.drain()
                vec.tensor_tensor(flat, flat,
                                  bc(gs_r.rearrange("p t g -> p (t g)").unsqueeze(2), TT * NG, EG), ALU.add)
                dve.drain()
                pick(O1)
                vec.scalar_tensor_tensor(out=sel_r, in0=O1, scalar=-1e30, in1=sel_r, op0=ALU.mult, op1=ALU.add)
                dve.drain()
                pick(O2)
                vec.tensor_tensor(hot_b, O1, O2, ALU.add).then_inc(s_hot, 1)
                for k, O in enumerate((O1, O2)):
                    vec.tensor_tensor(tmp_r, O, sc_r, ALU.mult)
                    dve.drain()
                    vec.tensor_reduce(wk[:, k, :], tmp_r, X_AX, ALU.add)
                    dve.drain()
                vec.tensor_tensor(gm_r, wk[:, 0, :], wk[:, 1, :], ALU.add)
                dve.drain()
                vec.reciprocal(gm_r, gm_r)
                dve.drain()
                vec.tensor_tensor(wk, wk, bc(gm_r.unsqueeze(1), 2, TT), ALU.mult)
                dve.wait_ge(pos_mm, layer + 1)
                pos = PS[:, 0, 0:TT * NE].rearrange("p (t e) -> p t e", t=TT)
                for k, O in enumerate((O1, O2)):
                    vec.tensor_tensor(tmp_r, O, pos, ALU.mult)
                    dve.drain()
                    vec.tensor_reduce(posk[:, k, :], tmp_r, X_AX, ALU.add)
                    dve.drain()
                vec.tensor_copy(cnt_f, PS[0:1, 1, 0:NE])
                vec.memset(rnd_f, 1.0)
                dve.drain()
                for r in range(1, RMAX):
                    vec.scalar_tensor_tensor(out=rnd_f, in0=cnt_f, scalar=float(SL * r), in1=rnd_f,
                                             op0=ALU.is_gt, op1=ALU.add)
                    dve.drain()
                vec.tensor_copy(rounds_i[0:1, layer, :], rnd_f)
                pk = posk.rearrange("p k t -> p (k t)")
                vec.tensor_tensor(ge, bc(pk.unsqueeze(2), 2 * TT, 9), bc(thr.unsqueeze(1), 2 * TT, 9), ALU.is_ge)
                dve.drain()
                qf = qm.rearrange("p k t -> p (k t)")
                vec.tensor_reduce(qf, ge[:, :, 1:9], X_AX, ALU.add)
                vec.tensor_tensor(rvv, ge[:, :, 0:8], ge[:, :, 1:9], ALU.subtract)
                dve.drain()
                vec.scalar_tensor_tensor(out=qf, in0=qf, scalar=-float(SL), in1=pk, op0=ALU.mult, op1=ALU.add)
                vec.tensor_tensor(rvv, rvv, bc(tokv.rearrange("p k t -> p (k t)").unsqueeze(2), 2 * TT, 8), ALU.mult)
                dve.drain()
                vec.tensor_tensor(Aoh, bc(io64.unsqueeze(1), 2 * TT, P), bc(qf.unsqueeze(2), 2 * TT, P), ALU.is_equal)
                dve.wait_ge(s_xnst, 64 * (layer + 1))
                for k, O in enumerate((O1, O2)):
                    for t in range(TT):
                        ins = vec.tensor_tensor(Boh[:, k, t, :].rearrange("p (e r) -> p e r", r=8),
                                                bc(O[:, t, :].unsqueeze(2), NE, 8),
                                                bc(rvv[:, TT * k + t, :].unsqueeze(1), NE, 8), ALU.mult)
                ins.then_inc(s_tab, 1)
                dve.wait_ge(tab_mm, layer + 1)
                raw = PS[:, 4, 0:NE * 8]
                vec.tensor_scalar(tabf, raw, -0.5, p4p, ALU.is_ge, ALU.mult)
                vec.memset(idx_i[:, NE * 8:NE * 8 + 8], int(BIG))
                dve.drain()
                vec.scalar_tensor_tensor(out=idx_i[:, 0:NE * 8], in0=raw, scalar=c1p, in1=tabf,
                                         op0=ALU.add, op1=ALU.add)
                dve.drain()
                vec.tensor_scalar(gidx_i, idx_i, 2, None, ALU.logical_shift_right).then_inc(s_idx, 1)
                dve.drain()

            def expert_round(n_norm, par, rows, mod, expo, hidden):
                dve.wait_ge(*rows)
                src = PS[:, par, :].rearrange("p (k s) -> p k s", k=KT)
                vec.tensor_tensor(xgT[:, par], src, bc(Acol[n_norm].unsqueeze(2), KT, SL), ALU.mult)
                dve.drain()
                vec.tensor_tensor(xgT[:, par], xgT[:, par], bc(Bcol[n_norm].unsqueeze(2), KT, SL), ALU.add)\
                    .then_inc(mod, 1)
                dve.wait_ge(*expo)
                h1, h3 = PS[:, 2, 0:256], PS[:, 2, 256:512]
                one_over_one_plus(hx[:, 0:256])
                dve.drain()
                vec.tensor_tensor(hx[:, 256:512], hx[:, 0:256], h1, ALU.mult)
                dve.drain()
                vec.tensor_tensor(hidb[:, par, :], hx[:, 256:512], h3, ALU.mult).then_inc(hidden, 1)

            def moe(layer):
                b = layer * NE
                n_norm = 2 * layer + 1
                router(layer)
                with dve.Fori(0, NE // 2) as it:
                    for u in range(2):
                        e = dve.snap(it * 2 + u, min_val=0, max_val=NE - 1)
                        rounds = dve.value_load(rounds_i[0:1, layer, ds(e, 1)], min_val=1, max_val=RMAX)
                        k = dve.snap(it * 2 + (b + u + 1), min_val=1, max_val=2 * NE)
                        expert_round(n_norm, u, (xt_mm, k), s_xt, (s_he, k), s_hid)
                        with dve.If(rounds > 1):
                            with dve.Fori(1, rounds) as r:
                                dve.reg_add(extra, extra, 1)
                                n = dve.snap(extra, min_val=1, max_val=2 * NE * RMAX)
                                expert_round(n_norm, u, (e_xt, n), e_sxt, (e_he, n), e_hid)
                                dve.wait_ge(e_st, n * 16)
                                settle(dve, idle)
                            dve.drain()
                        dve.drain()

            def combine(layer):
                dve.wait_ge(s_gB, 16 * (2 * layer + 2))
                for t in range(TT):
                    c = ct[t % 2]
                    dve.wait_ge(s_y0, layer * TT + t + 1)
                    vec.scalar_tensor_tensor(out=c, in0=yk[t % 2][:, 1, :], scalar=wk[:, 1, t:t + 1], in1=c,
                                             op0=ALU.mult, op1=ALU.add)
                    dve.drain()
                    vec.tensor_tensor(c, c, gB[:, :], ALU.mult)
                    dve.drain()
                    vec.tensor_tensor(X[:, t, :], X[:, t, :], c, ALU.add).then_inc(s_comb, 1)
                    dve.drain()

            extra = dve.alloc_register("dve_extra")
            dve.reg_mov(extra, 0)
            idle = dve.alloc_register("dve_idle")
            dve.reg_mov(idle, 0)
            add_output(0, 0)
            norm(1, mxn)
            moe(0)
            combine(0)

            norm(2, xn)
            dve.wait_ge(s_const, 3)
            for h in range(GH):
                dve.wait_ge(s_g1l, h + 1)
                g = lg_t[:, 0, :]
                vec.scalar_tensor_tensor(out=g, in0=g, scalar=0.0, in1=lg_t[:, 1, :], op0=ALU.min, op1=ALU.subtract)
                dve.drain()
                vec.tensor_scalar(g, g, 1.0 / GATE_TAU, None, ALU.mult)
                dve.drain()
                vec.tensor_tensor_scan(cum1[:, h, :], cmask[:, :], g, 0.0, ALU.mult, ALU.add).then_inc(s_cm, 1)
                dve.wait_ge(s_ec, h + 1)
                vec.scalar_tensor_tensor(out=q1[:, h, :], in0=q1[:, h, :], scalar=GDK ** -0.5, in1=lg_t[:, 0, :],
                                         op0=ALU.mult, op1=ALU.mult)
                vec.tensor_tensor(kend[:, h, :], k1[:, h, :], cum1[:, h, :], ALU.mult)
                dve.drain()
                vec.tensor_tensor(k1[:, h, :], k1[:, h, :], lg_t[:, 1, :], ALU.mult).then_inc(s_kend, 1)
                dve.drain()
            vec.memset(state, 0.0)
            dve.drain()

            def silu_tile(t):
                dve.wait_ge(s_rge, t + 1)
                one_over_one_plus(rexp[:, :])
                dve.drain()
                vec.tensor_tensor(r1[:, t, :], r1[:, t, :], rexp[:, :], ALU.mult).then_inc(s_silu, 1)
                dve.drain()

            def update_state(t, h, c):
                dve.wait_ge(oi_mm if c == 0 else o_mm, GH * t + h + 1)
                kv = PS[:, (6, 0)[c] + h // 2, (h % 2) * GDV:(h % 2 + 1) * GDV]
                vec.scalar_tensor_tensor(out=state[:, h, :], in0=state[:, h, :],
                                         scalar=dec1[:, h, 2 * t + c:2 * t + c + 1], in1=kv,
                                         op0=ALU.mult, op1=ALU.add).then_inc(s_st, 1)

            dve.wait_ge(s_small1, 48)
            for t in range(TT):
                silu_tile(t)
                dve.wait_ge(it_mm, t + 1)
                vec.tensor_tensor(itm, PS[:, 0, :].rearrange("p (h n) -> p h n", h=GH),
                                  bc(tri1[:, :].unsqueeze(1), GH, P), ALU.mult).then_inc(s_it, 1)
                for c in range(2):
                    dve.drain()
                    for h in range(GH):
                        update_state(t, h, c)
                dve.drain()
                dve.wait_ge(s_ors, t + 1)
                for h in range(GH):
                    ob = osb[:, h % 2, :]
                    vec.scalar_tensor_tensor(out=ob, in0=PS[:, 2 + h, 0:GDV], scalar=o_rs[:, h:h + 1], in1=ogain,
                                             op0=ALU.mult, op1=ALU.mult)
                    dve.drain()
                    y = r1[:, t, h * GDV:(h + 1) * GDV]
                    ins = vec.tensor_tensor(y, y, ob, ALU.mult)
                ins.then_inc(s_yo, 1)
                dve.drain()
            add_output(1, 2)
            norm(3, mxn)
            moe(1)
            combine(1)

        @block.tensor
        def _(pe):
            def mm(out, lhsT, rhs, first, last):
                return ten.matmul(out, lhsT, rhs, start=first, stop=last)

            def used(n=1):
                pe.drain()
                for _ in range(n):
                    ten.nop().then_inc(piece_used, 1)

            def adaln(g):
                if g:
                    pe.wait_ge(ada_row, g)
                for j in range(4):
                    landed(pe, ADA[g] + j)
                for kt in range(KT):
                    for j in range(4):
                        ins = mm(PS[32 * j:32 * j + 32, 4, :], keep_screp[:, kt, :], piece_ap(ADA[g] + j)[:, kt, :],
                                 kt == 0, kt == KT - 1)
                ins.then_inc(ada_mm, 1)
                used(4)

            def norm_transposes(n, xbuf):
                pe.wait_ge(s_xn, 4 * (n + 1))
                for kt in range(KT):
                    if kt >= 2:
                        pe.wait_ge(nt_v if kt % 2 else nt_a, 4 * n + kt // 2)
                    for t in range(TT):
                        src = xbuf[:, t, :].rearrange("p (q k) -> p k q", k=KT)[:, kt, :]
                        ins = ten.transpose(PS[:, 6 + kt % 2, t * P:(t + 1) * P], src, ident[:, :])
                    ins.then_inc(nt_mm, 1)
                pe.wait_ge(nt_a, 4 * (n + 1))
                pe.wait_ge(nt_v, 4 * (n + 1))

            def job0(n):
                if n >= 4:
                    pe.wait_ge(job_out, n - 3)
                out = PS[:, job_bank(n), :]
                if n:
                    piece, ct_ = WIN0[(n - 1) // 4], (n - 1) % 4
                    landed(pe, piece)
                for kt in range(KT):
                    if n == 0:
                        lhsT, rhs = wfx[:, kt, :], hT[:, kt, :]
                    elif n < 17:
                        lhsT, rhs = piece_ap(piece)[:, kt, ct_ * P:(ct_ + 1) * P], hT[:, kt, :]
                    else:
                        lhsT, rhs = hT[:, kt, ct_ * P:(ct_ + 1) * P], piece_ap(piece)[:, kt, :]
                    ins = mm(out, lhsT, rhs, kt == 0, kt == KT - 1)
                ins.then_inc(job_mm, 1)
                if n and ct_ == 3:
                    used()

            pe.wait_ge(s_const, 1)
            pe.wait_ge(s_pr, 16 * 12)
            ten.transpose(PS[:, 5, 0:NPC], prow, ident[0:NPC, 0:NPC]).then_inc(pr_mm, 1)
            pe.wait_ge(s_sc, 1)
            adaln(0)
            norm_transposes(0, xn)
            pe.wait_ge(s_fx, 16 * 6)
            for kind, i in ORDER0:
                if kind == "job":
                    job0(i)
                elif kind == "ada":
                    adaln(i)
                elif kind == "ri":
                    pe.wait_ge(s_xc, i + 1)
                    if i:
                        pe.wait_ge(s_ri, i)
                    mm(PS[:, 6, :], bd[:, 0, i, :], xc, True, True)
                    mm(PS[:, 7, :], bd[:, 1, i, :], xc, True, True).then_inc(ri_mm, 1)
                elif kind == "sn":
                    pe.wait_ge(s_sq, i + 1)
                    if i:
                        pe.wait_ge(s_rsb, i)
                    mm(PS[:, 5, :], blk64[:, :], sq[:, i % 2, :], True, True).then_inc(sn_mm, 1)

            def scores(n):
                h, t = divmod(n, TT)
                b, pr, N = 64 * (h % 2), h // 2, P * (t + 1)
                if n >= 4:
                    pe.wait_ge(s_ex, n - 3)
                out = PS[:, n % 4, 0:N]
                mm(out, qT[b:b + HD, pr, t * P:(t + 1) * P], kT[b:b + HD, pr, 0:N], True, False)
                mm(out, sel[b:b + HD, h, :], cumx[b:b + HD, 0:N], False, True).then_inc(sc_mm, 1)

            pe.wait_ge(job_out, JOBS0)
            pe.wait_ge(s_cum, 1)
            pe.wait_ge(s_qk, 8)
            pe.wait_ge(s_rsb, 8)
            pe.wait_ge(ada_row, 5)
            scores(0)
            scores(1)
            for n in range(HEADS * TT):
                h, t = divmod(n, TT)
                if n + 2 < HEADS * TT:
                    scores(n + 2)
                pe.wait_ge(s_pn, n + 1)
                if n >= 2:
                    pe.wait_ge(s_pt, n - 1)
                for kb in range(t + 1):
                    ins = ten.transpose(PS[:, 4 + n % 2, kb * P:(kb + 1) * P], prob[:, n % 2, kb * P:(kb + 1) * P],
                                        ident[:, :])
                ins.then_inc(pt_mm, 1)
                if n % 8 == 7:
                    pr = h // 2
                    pe.wait_ge(s_pt, n + 1)
                    if pr >= 2:
                        pe.wait_ge(s_yf, pr - 1)
                    for kb in range(TT):
                        for hh in range(2):
                            hd = 2 * pr + hh
                            ins = mm(PS[64 * hh:64 * hh + 64, 6 + pr % 2, kb * P:T],
                                     v_sb[:, kb, hd * HD:(hd + 1) * HD], pT[hh][:, kb, kb * P:T],
                                     kb == 0, kb == TT - 1)
                    ins.then_inc(pv_mm, 1)
            adaln(5)

            def output_projection(layer, bank0, first, lhs):
                for o in range(8):
                    half, t = divmod(o, TT)
                    if o == 0 or o == TT:
                        landed(pe, first[half])
                    if o >= 4:
                        pe.wait_ge(wo_x, 8 * layer + o - 3)
                    for kt in range(KT):
                        ins = mm(PS[:, bank0 + o % 4, :], lhs(kt, t), piece_ap(first[half])[:, kt, :],
                                 kt == 0, kt == KT - 1)
                    ins.then_inc(wo_mm, 1)
                    if t == TT - 1:
                        used()

            pe.wait_ge(s_yr, 4)
            pe.wait_ge(s_yf, 4)
            output_projection(0, 0, WOUT0, lambda kt, t: (
                xr[:, kt, 3 + t * P:3 + (t + 1) * P] if kt < 4 else yfT[:, kt - 4, t * P:(t + 1) * P]))

            def expert_round(slot, par, rows, xt, mod, hm, hidden, htm, moved, ym, weights):
                pe.wait_ge(*rows)
                ten.matmul(PS[:, 7, 0:1], ident[0:SL, :], ident[0:SL, 0:1], start=True, stop=True)
                for kt in range(KT):
                    src = xg[:, par, :].rearrange("p (q k) -> p k q", k=KT)[:, kt, :]
                    ins = ten.transpose(PS[:, par, kt * SL:(kt + 1) * SL], src, ident[0:SL, 0:SL])
                ins.then_inc(xt, 1)
                w13 = ring[:, slot:slot + 2, :].rearrange("p w (k f) -> p w k f", k=KT)
                w2 = ring[:, (slot + 2) % SLOTS, :].rearrange("p (h j n) -> p h j n", h=2, j=2)
                pe.wait_ge(*mod)
                weights(0)
                for kt in range(KT):
                    for half in range(2):
                        ins = mm(PS[SL * half:SL * half + SL, 2, :].rearrange("p (w f) -> p w f", w=2),
                                 xgT[:, par, kt, :], w13[:, :, kt, half * 256:(half + 1) * 256],
                                 kt == 0, kt == KT - 1)
                ins.then_inc(hm, 1)
                pe.wait_ge(*hidden)
                for j in range(2):
                    ins = ten.transpose(PS[:, 4, j * P:(j + 1) * P],
                                        hidb[:, par, :].rearrange("p (q j) -> p j q", j=2)[:, j, :], ident[:, :])
                ins.then_inc(htm, 1)
                pe.wait_ge(*moved)
                weights(1)
                for i in range(4):
                    h, j = divmod(i, 2)
                    for half in range(2):
                        ins = mm(PS[SL * half:SL * half + SL, 5 + par, :], hidT[:, par, j, h * SL:(h + 1) * SL],
                                 w2[:, h, j, half * NC:(half + 1) * NC], i == 0, i == 3)
                ins.then_inc(ym, 1)

            def moe(layer, first):
                b = layer * NE
                bg = layer * (NE + 1)
                for t in range(TT):
                    for kt in range(KT):
                        ins = mm(PS[:, 7, t * NE:(t + 1) * NE], hT[:, kt, t * P:(t + 1) * P], rw_sb[:, kt, :],
                                 kt == 0, kt == KT - 1)
                ins.then_inc(z_mm, 1)
                pe.wait_ge(s_hot, layer + 1)
                for t in range(TT):
                    for tp in range(t + 1):
                        mm(PS[:, 0, t * NE:(t + 1) * NE], triS if tp == t else ones_b, hot_b[:, tp, :],
                           tp == 0, tp == t)
                for t in range(TT):
                    ins = mm(PS[:, 1, 0:NE], ones_b, hot_b[:, t, :], t == 0, t == TT - 1)
                ins.then_inc(pos_mm, 1)
                pe.wait_ge(s_tab, layer + 1)
                for i in range(2 * TT):
                    ins = mm(PS[:, 4, 0:NE * 8], Aoh[:, i, :], Boh[:, i // TT, i % TT, :], i == 0, i == 2 * TT - 1)
                ins.then_inc(tab_mm, 1)
                pe.wait_ge(s_idx, layer + 1)
                with pe.Fori(0, NE // 2) as it:
                    for u in range(2):
                        e = pe.snap(it * 2 + u, min_val=0, max_val=NE - 1)
                        rounds = pe.value_load(rounds_i[0:1, layer, ds(e, 1)], min_val=1, max_val=RMAX)
                        k = pe.snap(it * 2 + (b + u + 1), min_val=1, max_val=2 * NE)
                        piece = first + 3 * u

                        def weights(part):
                            for p in ((piece, piece + 1), (piece + 2,))[part]:
                                pe.wait_ge(slot_in[slot_of(p)], it * 16 + 16 * (p // SLOTS + 1))
                        expert_round(slot_of(piece), u, (g_in, it * 32 + 16 * (bg + u + 1)), xt_mm, (s_xt, k), h_mm,
                                     (s_hid, k), ht_mm, (s_ht, k), y_mm, weights)
                        with pe.If(rounds > 1):
                            with pe.Fori(1, rounds) as r:
                                pe.reg_add(extra, extra, 1)
                                n = pe.snap(extra, min_val=1, max_val=2 * NE * RMAX)
                                expert_round(slot_of(piece), u, (e_g, n * 16), e_xt, (e_sxt, n), e_h, (e_hid, n),
                                             e_htm, (e_ht, n), e_ym, lambda part: None)
                                pe.wait_ge(e_st, n * 16)
                                settle(pe, idle)
                            pe.drain()
                        used(3)

            extra = pe.alloc_register("pe_extra")
            pe.reg_mov(extra, 0)
            idle = pe.alloc_register("pe_idle")
            pe.reg_mov(idle, 0)
            norm_transposes(1, mxn)
            moe(0, MOE0)

            norm_transposes(2, xn)
            pe.wait_ge(s_small1, 32)
            for kind, i in ORDER1:
                if kind == "g1":
                    pe.wait_ge(job_out, JOBS0 + 1)
                    if i >= 2:
                        pe.wait_ge(s_g1l, i - 1)
                    mm(PS[:, 4 + i % 2, :], wg2[:, i * P:(i + 1) * P], glow, True, True).then_inc(g1_mm, 1)
                    continue
                n = i
                if n >= 4:
                    pe.wait_ge(job_out, JOBS0 + n - 3)
                out = PS[:, job_bank(n), :]
                if n:
                    piece, ct_ = WIN1 + (n - 1) // 4, (n - 1) % 4
                    landed(pe, piece)
                for kt in range(KT):
                    if n == 0:
                        o_, lhsT, rhs = out[0:16, :], gw[:, kt, :], hT[:, kt, :]
                    elif n < 9:
                        o_, lhsT, rhs = out, piece_ap(piece)[:, kt, ct_ * P:(ct_ + 1) * P], hT[:, kt, :]
                    else:
                        o_, lhsT, rhs = out, hT[:, kt, ct_ * P:(ct_ + 1) * P], piece_ap(piece)[:, kt, :]
                    ins = mm(o_, lhsT, rhs, kt == 0, kt == KT - 1)
                ins.then_inc(job_mm, 1)
                if n and ct_ == 3:
                    used()

            def state_part(t, h, c):
                return ten.matmul(PS[c * CH:(c + 1) * CH, 2 + h, 0:GDV], q1[:, h, t * P + c * CH:t * P + (c + 1) * CH],
                                  state[:, h, :], start=False, stop=True, skip_group_check=True)

            pe.wait_ge(s_kend, GH)
            pe.wait_ge(job_out, JOBS0 + JOBS1)
            for t in range(TT):
                if t:
                    pe.wait_ge(s_yt, 2 * t)
                ts_ = slice(t * P, (t + 1) * P)
                for h in range(GH):
                    ins = mm(PS[:, 0, h * P:(h + 1) * P], k1[:, h, ts_], q1[:, h, ts_], True, True)
                ins.then_inc(it_mm, 1)
                for h in range(GH):
                    ins = ten.transpose(PS[:, 1, h * P:(h + 1) * P], kend[:, h, ts_], ident[:, :])
                ins.then_inc(ke_mm, 1)
                pe.wait_ge(s_ke, t + 1)
                pe.wait_ge(s_it, t + 1)
                for h in range(GH):
                    for c in range(2):
                        mm(PS[:, (6, 0)[c] + h // 2, (h % 2) * GDV:(h % 2 + 1) * GDV],
                           ketok[c * CH:(c + 1) * CH, h, :],
                           v1[c * CH:(c + 1) * CH, t, h * GDV:(h + 1) * GDV], True, True)
                for h in range(GH):
                    mm(PS[:, 2 + h, 0:GDV], itm[:, h, :], v1[:, t, h * GDV:(h + 1) * GDV], True, True)
                    if t:
                        pe.wait_ge(s_st, 2 * GH * (t - 1) + GH + h + 1)
                    state_part(t, h, 0).then_inc(oi_mm, 1)
                for h in range(GH):
                    pe.wait_ge(s_st, 2 * GH * t + h + 1)
                    state_part(t, h, 1).then_inc(o_mm, 1)
                pe.wait_ge(s_yo, t + 1)
                for kt in range(KT):
                    ins = ten.transpose(PS[:, kt // 4, kt % 4 * P:(kt % 4 + 1) * P], r1[:, t, kt * P:(kt + 1) * P],
                                        ident[:, :])
                    if kt % 4 == 3:
                        ins.then_inc(yt_mm, 1)
            pe.wait_ge(s_yt, 2 * TT)
            output_projection(1, 2, [WOUT1, WOUT1 + 1], lambda kt, t: yT1[:, kt, t * P:(t + 1) * P])
            norm_transposes(3, mxn)
            moe(1, MOE1)


_INS = ['x', 'c', 'router_w', 'router_b', 'ada_w', 'ada_b', 'norm_mix', 'norm_ffn', 'ev_w_in', 'ev_conv_w',
        'ev_conv_b', 'ev_r_w', 'ev_r_b', 'ev_i_w', 'ev_i_b', 'ev_lam', 'ev_forget_b', 'ev_q_gain', 'ev_k_gain',
        'ev_w_out', 'od_w_in', 'od_gate_w2', 'od_gate_b', 'od_out_gain', 'od_w_out', 'moe_w1', 'moe_w3', 'moe_w2']


def kernel(**inputs):
    import numpy as _np
    import concourse.bacc as _bacc
    from concourse import mybir as _mybir
    from concourse.bass_utils import run_bass_kernel_spmd as _run

    nc = _bacc.Bacc("TRN2", target_bir_lowering=False, num_devices=1)
    arrays, args = {}, {}
    for name in _INS:
        a = _np.ascontiguousarray(inputs[name])
        arrays[f"in_{name}"] = a
        args[name] = nc.dram_tensor(f"in_{name}", a.shape, _mybir.dt.from_np(a.dtype), kind="ExternalInput").ap()
    args["out"] = nc.dram_tensor("out_x", (1, T, D), _mybir.dt.float32, kind="ExternalOutput").ap()
    build_program(nc, args)
    r = _run(nc, [arrays], core_ids=[0])
    return r.results[0]["out_x"]
```

```python
import concourse.bass as bass
from concourse import mybir
from contextlib import ExitStack

P = 128
D = 1024
T = 512
TT = T // P
KT = D // P
NC = 512
HEADS = 8
HD = 64
EPS = 1e-6
GH, GDK, GDV = 4, 128, 256
CH = 64
NCH = T // CH
NE = 32
NG, EG = 4, 8
FE = 512
SL = 64
RMAX = T // SL
N_SMALL = 8
SLOTS = 6
PIECE = KT * NC
U = 4
BIG = 65536.0

RGLRU_C = 8.0
GATE_TAU = 16.0
WIN0 = [4, 5, 10, 15, 20]
WOUT0 = [21, 22]
MOE0 = 27
WIN1 = MOE0 + 3 * NE + 4
ADA = [0, 6, 11, 16, 23, WIN1 - 4]
WOUT1 = WIN1 + 6
MOE1 = WOUT1 + 2


def build_program(nc, A):
    F32, I32, BF16 = mybir.dt.float32, mybir.dt.int32, mybir.dt.bfloat16
    ALU = mybir.AluOpType
    ACT = mybir.ActivationFunctionType
    X_AX = mybir.AxisListType.X
    ds = bass.ds
    vec, act_, pool_, ten = nc.vector, nc.scalar, nc.gpsimd, nc.tensor

    ctx = ExitStack()
    with ctx:
        def sb(name, shape, dt=F32):
            return ctx.enter_context(nc.sbuf_tensor(name, shape, dt))

        def sem(name):
            return ctx.enter_context(nc.semaphore(name))

        mod_d = nc.dram_tensor("mod_d", (2, 12, NC), F32).ap()
        xn_d = [nc.dram_tensor(f"xn_d{l}", (T, D), F32).ap() for l in range(2)]
        credit_d = nc.dram_tensor("credit_d", (U + 1, P, 1), F32).ap()
        y_d = [nc.dram_tensor(f"y_d{l}", (T * 4, NC), F32).ap() for l in range(2)]

        X = sb("X", [P, TT, D])
        hT = sb("hT", [P, KT, T])
        ring = sb("ring", [P, SLOTS, PIECE])
        S = sb("S", [P, 16400])
        ident = sb("ident", [P, P])
        maskneg = sb("maskneg", [P, P])
        blk64 = sb("blk64", [P, P])
        sel = sb("sel", [P, HEADS, P])
        cumx = sb("cumx", [P, T])
        rw_sb = sb("rw_sb", [P, KT, NE])
        gB = sb("gB", [P, D])
        cols = sb("cols", [P, 300])
        rounds_i = sb("rounds_i", [1, 2, NE + U], I32)

        def carve(base, *shape, parts=P, of=None):
            n = 1
            for s in shape:
                n *= s
            v = (S if of is None else of)[0:parts, base:base + n]
            if len(shape) == 1:
                return v
            names = "abcd"[:len(shape)]
            return v.rearrange(f"p ({' '.join(names)}) -> p {' '.join(names)}",
                               **{k: s for k, s in zip(names[1:], shape[1:])})

        hT_flat = hT[:, :, :].rearrange("p k t -> p (k t)")
        XR_W = T + 4
        xr = carve(0, 4, XR_W)
        gate = carve(4 * XR_W, 4, T)
        qT = carve(4 * XR_W + 2048, 4, T)
        part0 = [qT[:, j, :] for j in range(4)]
        kT = carve(4 * XR_W + 4096, 4, T)
        V0 = 4 * XR_W + 6144
        v_sb = carve(V0, TT, 512)
        wfx = carve(V0, KT, P)
        bd = carve(V0 + 1024, 2, 4, P)
        T0 = V0 + 2048
        xn = carve(T0, TT, D)
        xc = carve(T0, T)
        ri = carve(T0 + 512, 2, T)
        ra = carve(T0 + 1536, T)
        rt = carve(T0 + 2048, T)
        ru = carve(T0 + 2560, T)
        sq = carve(T0 + 3072, 2, T)
        rstd_b = carve(T0 + 4096, 2, T)
        modrow = carve(T0 + 5120, NC)
        biasrow = carve(T0 + 5632, NC)
        prob = carve(T0, 2, T)
        pT = [carve(T0 + 1024, 4, T), carve(2048, 4, T, of=hT_flat)]
        yfT = carve(0, 4, T, of=hT_flat)
        out_tmp = carve(T0 + 4608, NC)
        qz = carve(T0 + 4608, 2, 2, P)
        kz = [carve(T0 + 3072, 2, T), carve(T0 + 5120, 2, T)]

        _c = [0]

        def col(n):
            _c[0] += n
            return cols[:, _c[0] - n:_c[0]]
        cT, cE = col(KT), col(KT)
        ssq, rstd = col(TT), col(TT)
        gain_mf = [col(KT) for _ in range(4)]
        Acol = [col(KT) for _ in range(4)]
        Bcol = [col(KT) for _ in range(4)]
        rbB = col(NE)
        lastc = col(NCH)
        convw, convb, rb_c, ib_c, lamc, gbias = col(16), col(4), col(4), col(4), col(4), col(4)
        qg, kg, fb = col(1), col(1), col(1)
        NPC = 39
        pcols = cols[:, _c[0] - NPC:_c[0]]
        prow = gB[0:NPC, 0:P]
        nsp8, sp_t, lw = col(4), col(4), col(4)
        nmx, rsum, rinv = col(4), col(4), col(4)
        partc, c1p, p4p, idlec = col(1), col(1), col(1), col(3)
        sel4, idle_c = col(1), col(1)
        sel_sum = col(NE)
        eps_c = col(1)
        keep_screp = sb("screp", [P, KT, 32])
        PS = ctx.enter_context(nc.psum_tensor("PS", [P, 8, 512], F32))

        slot_in = [sem(f"slot_in{i}") for i in range(SLOTS)]
        piece_used = sem("piece_used")
        ada0_mm = sem("ada0_mm")
        s_part = sem("s_part")
        s_sel4 = sem("s_sel4")
        col_mm = sem("col_mm")
        s_h0 = sem("s_h0")
        s_pr = sem("s_pr")
        pr_mm = sem("pr_mm")
        s_prep = sem("s_prep")
        s_c = sem("s_c")
        s_ce = sem("s_ce")
        s_lamx = sem("s_lamx")
        moe_done = sem("moe_done")
        s_silu = sem("s_silu")
        s_kend = sem("s_kend")
        ke_mm = sem("ke_mm")
        oi_mm = sem("oi_mm")
        o_mm = sem("o_mm")
        s_small = sem("s_small")
        s_fx = sem("s_fx")
        s_x = [sem(f"s_x{t}") for t in range(TT)]
        s_const = sem("s_const")
        s_sc = sem("s_sc")
        ada_mm = sem("ada_mm")
        ada_row = sem("ada_row")
        ada_bias = sem("ada_bias")
        ada_st = sem("ada_st")
        s_mod = sem("s_mod")
        s_gB = sem("s_gB")
        s_ab = sem("s_ab")
        s_rstd = sem("s_rstd")
        s_xn = sem("s_xn")
        s_xnst = sem("s_xnst")
        nt_mm = sem("nt_mm")
        nt_a = sem("nt_a")
        nt_v = sem("nt_v")
        zt_mm = sem("zt_mm")
        s_zt = sem("s_zt")
        job_mm = sem("job_mm")
        job_out = sem("job_out")
        s_sq = sem("s_sq")
        sn_mm = sem("sn_mm")
        s_rsb = sem("s_rsb")
        s_qk = sem("s_qk")
        s_xc = sem("s_xc")
        ri_mm = sem("ri_mm")
        s_ri = sem("s_ri")
        s_at = sem("s_at")
        s_v = sem("s_v")
        s_sqv = sem("s_sqv")
        s_gz = sem("s_gz")
        s_ge = sem("s_ge")
        s_yr = sem("s_yr")
        s_lamE = sem("s_lamE")
        s_lamL = sem("s_lamL")
        s_fl = sem("s_fl")
        s_cum = sem("s_cum")
        s_kz0 = sem("s_kz0")
        s_qz = sem("s_qz")
        sc_mm = sem("sc_mm")
        s_mx = sem("s_mx")
        s_ex = sem("s_ex")
        s_pn = sem("s_pn")
        pt_mm = sem("pt_mm")
        s_pt = sem("s_pt")
        pv_mm = sem("pv_mm")
        s_yf = sem("s_yf")
        wo_mm = sem("wo_mm")
        wo_x = sem("wo_x")
        z_mm = sem("z_mm")
        s_ez = sem("s_ez")
        s_hot = sem("s_hot")
        pos_mm = sem("pos_mm")
        s_tab = sem("s_tab")
        tab_mm = sem("tab_mm")
        s_idx = sem("s_idx")
        g_hi = [sem(f"g_hi{i}") for i in range(U)]
        g_in = [sem(f"g_in{i}") for i in range(U)]
        xt_mm = sem("xt_mm")
        s_xt = sem("s_xt")
        h_mm = sem("h_mm")
        s_he = sem("s_he")
        s_hid = sem("s_hid")
        ht_mm = sem("ht_mm")
        s_ht = sem("s_ht")
        y_mm = sem("y_mm")
        s_y = sem("s_y")
        y_st = [sem(f"y_st{i}") for i in range(U)]
        ticks, extra_ticks, end_ticks = sem("ticks"), sem("extra_ticks"), sem("end_ticks")
        s_ecur = sem("s_ecur")
        e_g, e_xt, e_sxt, e_h, e_he, e_hid, e_htm, e_ht, e_ym, e_y, e_st = (
            sem("extra_" + n) for n in ("gather", "xt_mm", "xt", "h_mm", "he", "hid", "ht_mm", "ht", "y_mm", "y", "st"))
        y_in = [sem(f"y_in{t}") for t in range(TT)]
        s_y0 = sem("s_y0")
        s_comb = sem("s_comb")
        s_out = sem("s_out")
        s_small1 = sem("s_small1")
        g1_mm = sem("g1_mm")
        s_g1l = sem("s_g1l")
        s_cm = sem("s_cm")
        s_ec = sem("s_ec")
        it_mm = sem("it_mm")
        s_it = sem("s_it")
        s_ke = sem("s_ke")
        s_kz = sem("s_kz")
        s_st = sem("s_st")
        s_ors = sem("s_ors")
        s_yo = sem("s_yo")
        yt_mm = sem("yt_mm")
        s_yt = sem("s_yt")
        block = ctx.enter_context(nc.Block())

        ada_v = A["ada_w"].rearrange("l (p k) n -> l p k n", k=KT)
        win0_v = A["ev_w_in"].rearrange("a (p k) n -> (a p) k n", k=KT)
        wout0_v = A["ev_w_out"].rearrange("a (k p) n -> (a p) k n", p=P)
        win1_v = A["od_w_in"].rearrange("a (p k) n -> (a p) k n", k=KT)
        wout1_v = A["od_w_out"].rearrange("a (k p) n -> (a p) k n", p=P)
        w1_v = A["moe_w1"].rearrange("l e (p k) f -> (l e) p (k f)", k=KT)
        w3_v = A["moe_w3"].rearrange("l e (p k) f -> (l e) p (k f)", k=KT)
        w2_v = A["moe_w2"].rearrange("l e (h p j) n -> (l e) p h (j n)", h=2, j=2)
        x_v = A["x"].rearrange("b (t p) d -> (b p) t d", p=P)
        out_v = A["out"].rearrange("b (t p) d -> (b p) t d", p=P)
        adab_v = A["ada_b"].rearrange("l (c n) -> (l c) n", n=NC)
        modr = mod_d.rearrange("l c n -> (l c) n")

        def mod_vec(l, which):
            return mod_d[l, 2 * which:2 * which + 2, :]

        def slot_of(piece):
            return piece % SLOTS

        def landed(eng, piece):
            eng.wait_ge(slot_in[piece % SLOTS], 16 * (piece // SLOTS + 1))

        def head_tile(n):
            return 2 * (n // (2 * TT)) + n % 2, n // 2 % TT

        def settle(eng, reg):
            eng.reg_add(reg, reg, 1)

        def piece_ap(piece):
            return ring[:, slot_of(piece), :].rearrange("p (k n) -> p k n", k=KT)

        @block.sync
        def _(sp):
            def load(piece, src):
                if piece >= SLOTS:
                    sp.wait_ge(piece_used, piece - SLOTS + 1)
                dst = piece_ap(piece)
                if len(src.shape) == 2:
                    dst = ring[:, slot_of(piece), :]
                sp.dma_start(dst, src).then_inc(slot_in[slot_of(piece)], 16)

            def stream_experts(layer, first):
                with sp.Fori(0, NE // U) as it:
                    for u in range(U):
                        e = sp.snap(it * U + (layer * NE + u), min_val=0, max_val=2 * NE - 1)
                        for j, w in enumerate((w1_v, w3_v, w2_v)):
                            piece = first + 3 * u + j
                            slot = slot_of(piece)
                            sp.wait_ge(piece_used, it * (3 * U) + (piece - SLOTS + 1))
                            if j < 2:
                                sp.dma_start(ring[:, slot, :], w[ds(e, 1)].rearrange("a p n -> (a p) n"))\
                                    .then_inc(slot_in[slot], 16)
                            else:
                                sp.dma_start(ring[:, slot, :].rearrange("p (h m) -> p h m", h=2),
                                             w[ds(e, 1)].rearrange("a p h m -> (a p) h m"))\
                                    .then_inc(slot_in[slot], 16)

            def load_ada(g):
                for j in range(4):
                    c = (4 * g + j) % 12
                    load(ADA[g] + j, ada_v[g // 3, :, :, c * NC:(c + 1) * NC])

            def load_in0(c):
                load(WIN0[c], win0_v[:, :, c * NC:(c + 1) * NC])
            for t in range(TT):
                sp.dma_start(X[:, t, :], x_v[:, t, :]).then_inc(s_x[t], 16)
            load_ada(0)
            small = [(gain_mf[2 * l + f], A[("norm_mix", "norm_ffn")[f]][l:l + 1, :].rearrange("a (p k) -> (a p) k", k=KT))
                     for l in range(2) for f in range(2)]
            small += [(dst, A["ada_b"][0:1, w * D:(w + 1) * D].rearrange("a (p k) -> (a p) k", k=KT))
                      for w, dst in enumerate((Bcol[0], Acol[0]))]
            small += [(rw_sb[:, :, :], A["router_w"].rearrange("(p k) e -> p k e", k=KT)),
                      (rbB, A["router_b"].partition_broadcast(P))]
            for dst, src in small:
                sp.dma_start(dst, src).then_inc(s_small, 16)
            assert len(small) == N_SMALL
            sp.wait_ge(s_const, 1)
            for o in (0, 64):
                sp.dma_start(wfx[:, :, o:o + HEADS], win0_v[:, :, 2560:2568]).then_inc(s_fx, 16)
            for g, name in enumerate(("ev_r_w", "ev_i_w")):
                wv = A[name].rearrange("a (c b) d e -> b (a d) c e", b=2)
                for b in range(2):
                    sp.dma_start(bd[64 * b:64 * b + 64, g, :, 64 * b:64 * b + 64], wv[b]).then_inc(s_fx, 16)
            sp.wait_ge(s_pr, 16 * 12)
            sp.wait_ge(s_fx, 16 * 6)
            load_in0(0)
            load_in0(1)
            for c in range(2, 5):
                load_ada(c - 1)
                load_in0(c)
            for c in range(2):
                load(WOUT0[c], wout0_v[:, :, c * NC:(c + 1) * NC])
            load_ada(4)
            stream_experts(0, MOE0)
            sp.wait_ge(y_in[1], 16)
            load_ada(5)
            for n, c in enumerate((0, 1, 4, 5, 2, 3)):
                load(WIN1 + n, win1_v[:, :, c * NC:(c + 1) * NC])
            for c in range(2):
                load(WOUT1 + c, wout1_v[:, :, c * NC:(c + 1) * NC])
            stream_experts(1, MOE1)

        mxn = [carve(4 * XR_W + 2048, TT, D), carve(0, TT, D)]
        xg = carve(0, U, D)
        xg_e = carve(4096, D, parts=SL)
        ysb = [carve(5120, NC), carve(5632, NC), carve(8704, NC), carve(9216, NC)]
        ysb_e = carve(2048, NC, of=hT_flat)
        xgT = carve(6144, 2, KT, SL)
        hx = carve(7168, 2 * FE // 2)
        hidb = carve(7680, 2, 256)
        hidT = carve(8192, 2, 2, P)
        xgT_e = carve(2560, KT, SL, of=hT_flat)
        hx_e = carve(3072, FE, of=hT_flat)
        hidb_e = carve(3584, 256, of=hT_flat)
        hidT_e = carve(3840, 2, P, of=hT_flat)
        RB = 9728
        sc_r = carve(RB, TT, NE)
        sel_r = carve(RB + 128, TT, NE)
        tmp_r = carve(RB + 256, TT, NE)
        O1 = carve(RB + 384, TT, NE)
        O2 = carve(RB + 512, TT, NE)
        zT = carve(RB + 2140 + 64, T)
        wE = carve(RB + 672, NE)
        wG = carve(RB + 704, NG)
        thr = carve(RB + 708, 9)
        top8 = carve(RB + 720, TT * NG, 8)
        gs_r = carve(RB + 848, TT, NG)
        gm_r = carve(RB + 864, TT)
        gv_r = carve(RB + 868, TT, NG)
        wk = col(2 * TT).rearrange("p (k t) -> p k t", k=2)
        assert _c[0] <= 300
        posk = carve(RB + 892, 2, TT)
        ge = carve(RB + 900, 8, 9)
        qm = carve(RB + 972, 2, TT)
        tokv = carve(RB + 980, 2, TT)
        io64 = carve(RB + 988, P)
        Aoh = carve(RB + 1116, 2 * TT, P)
        rvv = carve(RB + 2140, 2 * TT, 8)
        Boh = carve(0, 2, TT, NE * 8, of=hT_flat)
        hot_b = carve(RB + 3228, TT * NE // 2).bitcast(BF16).rearrange("p (t e) -> p t e", t=TT)
        triS = carve(RB + 3292, P // 2).bitcast(BF16)
        ones_b = carve(RB + 3356, P // 2).bitcast(BF16)
        NIDX = (NE + U) * 8
        idx_i = carve(RB + 3420, NIDX).bitcast(I32)
        gidx_i = carve(RB + 3420 + NIDX, NIDX).bitcast(I32)
        RC = RB + 3420 + 2 * NIDX
        icur = [carve(RC + i, 1).bitcast(I32) for i in range(U)]
        gcur = [carve(RC + U + i, 1).bitcast(I32) for i in range(U)]
        ghi = [carve(RC + 330 + i, 1).bitcast(I32) for i in range(U)]
        icur_e = carve(RC + 2 * U, 1).bitcast(I32)
        gcur_e = carve(RC + 2 * U + 1, 1).bitcast(I32)
        tabf = carve(RC + 10, NE * 8)
        cnt_f = carve(RC + 266, NE, parts=1)
        rnd_f = carve(RC + 298, NE, parts=1)
        yk = [carve(2 * D * t, 2, D) for t in range(TT)]
        ct = [carve(2 * D * TT, D), carve(2 * D * TT + D, D)]
        assert RC + 330 + U <= 16400

        q1 = carve(0, GH, T)
        k1 = carve(2048, GH, T)
        v1 = carve(4096, TT, D)
        r1 = carve(8192, TT, D)
        cum1 = carve(12288, GH, T)
        state = carve(14336, GH, GDV)
        lg_t = carve(14336, 2, T)
        itm = sel[:, 0:4, :]
        ketok = [sel[:, 4:8, :], carve(15360, GH, P)]
        ogain = carve(15872, GDV)
        dec1 = carve(16128, GH, NCH)
        tri1 = maskneg
        kend = cum1
        cmask = cumx
        rexp = gB
        yT1 = hT
        wg2 = sel[0:16, 0:4, :].rearrange("p a b -> p (a b)")
        glow = sel[0:16, 4:8, :].rearrange("p a b -> p (a b)")
        gw = blk64[:, :].rearrange("p (k n) -> p k n", k=KT)
        o_ss, o_rs = nmx, rsum

        @block.gpsimd
        def _(pool):
            for m in (ident, maskneg, blk64):
                pool_.memset(m[:, :], 0.0)
            pool_.memset(sel[:, :, :], 0.0)
            pool_.memset(carve(V0, 2048), 0.0)
            pool_.memset(xr[:, :, 0:3], 0.0)
            pool_.memset(gB[0:64, 0:P], 0.0)
            pool_.memset(eps_c, EPS)
            pool.drain()
            pool_.affine_select(out=ident[:, :], in_=ident[:, :], compare_op=ALU.not_equal, fill=1.0, base=0,
                                pattern=[[-1, P]], channel_multiplier=1)
            pool_.affine_select(out=maskneg[:, :], in_=maskneg[:, :], compare_op=ALU.is_ge, fill=-1e30, base=0,
                                pattern=[[-1, P]], channel_multiplier=1)
            pool.drain()
            for o in (0, HD):
                pool_.memset(blk64[o:o + HD, o:o + HD], 1.0)
                pool.drain()
            for base in (0, -64):
                pool_.affine_select(out=sel[:, :, :], in_=sel[:, :, :], compare_op=ALU.not_equal, fill=-1.0,
                                    base=base, pattern=[[-1, HEADS], [0, P]], channel_multiplier=1)
                pool.drain()
            pool_.iota(partc, [[0, 1]], base=0, channel_multiplier=1, allow_small_or_imprecise_dtypes=True)
            pool.drain()
            pool_.tensor_scalar(c1p, partc, 63.5, BIG, ALU.is_gt, ALU.add)
            pool_.tensor_scalar(p4p, partc, 4.0, None, ALU.mult)
            pool.drain()
            pool_.nop().then_inc(s_const, 1)
            pool_.nop().then_inc(e_y, 1)
            pool_.nop().then_inc(ticks, 1)
            pool_.nop().then_inc(extra_ticks, 2)
            row = 0
            for name in ("ev_conv_w", "ev_conv_b", "ev_r_b", "ev_i_b", "ev_lam", "od_gate_b"):
                n = A[name].size() // P
                dims = {2: "a (c p) -> (a c) p", 3: "a j (c p) -> (a j c) p"}
                src = A[name].rearrange(dims[len(A[name].shape)], p=P) if A[name].shape[-1] != HD else \
                    A[name].rearrange("a (c b) e -> (a c) (b e)", b=2)
                pool.dma_start(prow[row:row + n, :], src).then_inc(s_pr, 16)
                row += n
            for o in (0, HD):
                for r, name in enumerate(("ev_q_gain", "ev_k_gain", "ev_forget_b")):
                    pool.dma_start(prow[row + r:row + r + 1, o:o + A[name].size()], A[name]).then_inc(s_pr, 16)

            for i, credit in enumerate((*y_st, e_st)):
                pool.dma_start(credit_d[i], partc).then_inc(credit, 16)

            def router_consts(layer):
                pool.wait_ge(wo_x, 8 * (layer + 1))
                pool_.iota(wE, [[-1, NE]], base=NE, channel_multiplier=0, allow_small_or_imprecise_dtypes=True)
                pool_.iota(wG, [[-1, NG]], base=NG, channel_multiplier=0, allow_small_or_imprecise_dtypes=True)
                pool_.iota(thr, [[SL, 9]], base=0, channel_multiplier=0, allow_small_or_imprecise_dtypes=True)
                pool_.iota(io64, [[0, 2], [1, SL]], base=0, channel_multiplier=0, allow_small_or_imprecise_dtypes=True)
                pool_.iota(tokv, [[2, 2], [4 * P, TT]], base=-int(BIG), channel_multiplier=4,
                           allow_small_or_imprecise_dtypes=True)
                pool_.memset(ones_b, 1.0)
                pool_.memset(triS, 0.0)
                if layer == 0:
                    pool_.memset(S[:, 0:4 * XR_W + 2048], 0.0)
                else:
                    pool_.memset(xg_e, 0.0)
                pool.drain()
                pool_.affine_select(out=triS, in_=triS, compare_op=ALU.is_ge, fill=1.0, base=0,
                                    pattern=[[-1, P]], channel_multiplier=1)
                pool.drain()
                pool_.nop().then_inc(s_const, 1)

            def tick(place, ticks):
                pool_.tensor_tensor(idlec[:, place:place + 1], partc, partc, ALU.add).then_inc(ticks, 1)

            def gather(layer, rows, index, done):
                pool_.indirect_dma_start(rows, None, xn_d[layer], bass.IndirectOffsetOnAxis(index, 0),
                                         bounds_check=T - 1, oob_is_err=False).then_inc(done, 16)

            def scatter(layer, result, index, done):
                pool_.indirect_dma_start(y_d[layer], bass.IndirectOffsetOnAxis(index[:, 0:1], 0),
                                         result, None,
                                         bounds_check=4 * T - 1, oob_is_err=False).then_inc(done, 16)

            extra = pool.alloc_register("pool_extra")
            pool.reg_mov(extra, 0)
            deep = pool.alloc_register("pool_deep")
            pool.reg_mov(deep, 0)

            def moe(layer):
                b = layer * NE
                before = layer * (NE + U) // U
                pool.wait_ge(s_idx, layer + 1)
                for u in range(U):
                    gather(layer, xg[0:SL, u, :], gcur[u][0:SL, 0:1], g_in[u])
                    rounds = pool.value_load(rounds_i[0:1, layer, u:u + 1], min_val=1, max_val=RMAX)
                    with pool.If(rounds > 1):
                        gather(layer, xg[SL:P, u, :], ghi[u][0:SL, 0:1], g_hi[u])
                with pool.Fori(0, NE // U) as it:
                    for u in range(U):
                        e = pool.snap(it * U + u, min_val=0, max_val=NE - 1)
                        rounds = pool.value_load(rounds_i[0:1, layer, ds(e, 1)], min_val=1, max_val=RMAX)
                        k = pool.snap(it * U + (b + u), min_val=0, max_val=2 * NE)
                        with pool.If(rounds > 1):
                            with pool.If(rounds > 2):
                                with pool.Fori(2, rounds) as r:
                                    pool.reg_add(extra, extra, 1)
                                    pool.reg_add(deep, deep, 1)
                                    n = pool.snap(extra, min_val=1, max_val=2 * NE * RMAX)
                                    d = pool.snap(deep, min_val=1, max_val=2 * NE * RMAX)
                                    pool.wait_ge(s_ecur, k + d)
                                    pool.wait_ge(extra_ticks, n + d)
                                    tick(1, extra_ticks)
                                    gather(layer, xg_e, gcur_e[0:SL, 0:1], e_g)
                                    pool.wait_ge(e_y, n + 1)
                                    pool.wait_ge(extra_ticks, n + d + 1)
                                    tick(1, extra_ticks)
                                    scatter(layer, ysb_e, icur_e, e_st)
                            pool.reg_add(extra, extra, 1)
                            n = pool.snap(extra, min_val=1, max_val=2 * NE * RMAX)
                            d = pool.snap(deep, min_val=0, max_val=2 * NE * RMAX)
                            pool.wait_ge(e_y, n + 1)
                            pool.wait_ge(extra_ticks, n + d + 1)
                            tick(1, extra_ticks)
                            scatter(layer, ysb_e, icur_e, e_st)
                        pool.wait_ge(s_y, it * U + (b + u + 1))
                        pool.wait_ge(ticks, k + 1)
                        tick(0, ticks)
                        scatter(layer, ysb[u], icur[u], y_st[u])
                        gather(layer, xg[0:SL, u, :], gcur[u][0:SL, 0:1], g_in[u])
                        later = pool.value_load(rounds_i[0:1, layer, ds(e + U, 1)], min_val=1, max_val=RMAX)
                        with pool.If(later > 1):
                            gather(layer, xg[SL:P, u, :], ghi[u][0:SL, 0:1], g_hi[u])
                for u in range(U):
                    pool.wait_ge(g_in[u], 16 * (before + NE // U + 1))
                    pool.wait_ge(y_st[u], 16 * (1 + (layer + 1) * NE // U))
                n = pool.snap(extra, min_val=0, max_val=2 * NE * RMAX)
                pool.wait_ge(e_st, n * 16 + 16)
                tick(2, end_ticks)
                pool.drain()
                pool_.nop().then_inc(moe_done, 1)

            def load_rows(layer):
                yv = y_d[layer].rearrange("(t p c) n -> t p (c n)", p=P, c=4)
                for t in range(TT):
                    pool.dma_start(yk[t].rearrange("p a n -> p (a n)"), yv[t]).then_inc(y_in[t], 16)

            def adaln_bias(g):
                for j in range(4):
                    pool.dma_start(biasrow[32 * j:32 * j + 32, :],
                                   adab_v[4 * g + j:4 * g + j + 1, :].partition_broadcast(32)
                                   .rearrange("p a n -> p (a n)")).then_inc(ada_bias, 16)

            def adaln_sum(g):
                pool.wait_ge(ada_bias, 64 * g)
                pool.wait_ge(ada_row, g)
                pool_.tensor_tensor(modrow, modrow, biasrow, ALU.add)
                pool.drain()
                pool.dma_start(modr[4 * g:4 * g + 4, :], modrow[0:P:32, :]).then_inc(ada_st, 16)

            def adaln_out(g):
                adaln_bias(g)
                adaln_sum(g)
                pool.wait_ge(ada_st, 16 * g)

            def load_mod(n):
                layer, ffn = n // 2, n % 2
                for dst, which in ((Bcol[n], 3 * ffn), (Acol[n], 3 * ffn + 1)):
                    pool.dma_start(dst, mod_vec(layer, which).rearrange("c (q k) -> (c q) k", k=KT))\
                        .then_inc(s_mod, 16)

            def load_gate(layer, ffn):
                src = mod_vec(layer, 3 * ffn + 2).rearrange("c n -> (c n)")
                pool.dma_start(gB[:, :], src.partition_broadcast(P)).then_inc(s_gB, 16)

            def store_xn(layer):
                for t in range(TT):
                    pool.wait_ge(s_xn, 4 * (2 * layer + 1) + t + 1)
                    pool.dma_start(xn_d[layer][t * P:(t + 1) * P, :], mxn[layer][:, t, :]).then_inc(s_xnst, 16)
                pool.wait_ge(s_xnst, 64 * (layer + 1))

            def qk_scale(m):
                pool.wait_ge(s_rsb, m + 1)
                dst = (qT if m < 4 else kT)[:, m % 4, :]
                pool_.tensor_tensor(dst, dst, rstd_b[:, m % 2, :], ALU.mult).then_inc(s_qk, 1)

            adaln_out(1)
            load_gate(0, 0)
            for m in range(3):
                qk_scale(m)
            adaln_out(2)
            load_mod(1)
            for m in range(3, 7):
                qk_scale(m)
            adaln_out(3)
            load_mod(2)
            qk_scale(7)
            pool.wait_ge(s_rsb, 8)
            pool.drain()
            for n in range(HEADS * TT):
                h, t = head_tile(n)
                own = slice(HD * (h % 2), HD * (h % 2) + HD)
                other = slice(HD - HD * (h % 2), P - HD * (h % 2))
                if n >= 4:
                    pool.wait_ge(sc_mm, n - 3)
                if t == 0 and h >= 2:
                    if h >= 4:
                        pool.wait_ge(sc_mm, 8 * (h // 2) - 8)
                    pool_.tensor_copy(kz[h % 2][own, h // 2 % 2, :], kT[own, h // 2, :])
                if t < 2:
                    pool_.tensor_copy(qz[other, n % 2, n // 2 % 2, :], sel[other, h, :])
                pool_.tensor_copy(qz[own, n % 2, n // 2 % 2, :], qT[own, h // 2, t * P:(t + 1) * P])
                pool.drain()
                pool_.nop().then_inc(s_qz, 1)
            pool.wait_ge(sc_mm, HEADS * TT)
            adaln_bias(4)
            router_consts(0)
            load_gate(0, 1)
            pool.dma_start(gw, win1_v[:, :, 3072:3088]).then_inc(s_small1, 16)
            pool.dma_start(wg2, A["od_gate_w2"].rearrange("a r n -> (a r) n")).then_inc(s_small1, 16)
            pool_.memset(cmask[:, :], 1.0)
            pool.drain()
            pool_.memset(cmask[:, :].rearrange("p (n c) -> p n c", c=CH)[:, :, 0:1], 0.0)
            pool_.memset(tri1[:, :], 1.0)
            pool.drain()
            pool_.affine_select(out=tri1[:, :], in_=tri1[:, :], compare_op=ALU.is_ge, fill=0.0, base=0,
                                pattern=[[1, P]], channel_multiplier=-1)
            pool.drain()
            pool_.memset(tri1[0:CH, CH:P], 0.0)
            pool.drain()
            pool_.nop().then_inc(s_const, 1)
            store_xn(0)
            adaln_sum(4)
            moe(0)
            load_rows(0)
            pool.wait_ge(ada_st, 16 * 4)
            adaln_out(5)
            load_mod(3)
            pool.wait_ge(s_comb, TT)
            pool.dma_start(ogain, A["od_out_gain"].rearrange("a n -> (a n)").partition_broadcast(P))\
                .then_inc(s_small1, 16)
            pool.wait_ge(s_silu, 2 * TT)
            load_gate(1, 0)
            router_consts(1)
            load_gate(1, 1)
            store_xn(1)
            moe(1)
            load_rows(1)

        def q_job(m):
            return ("job", 9 + m)
        ORDER0 = ([("job", 0), ("lam", 0)] + [("job", n) for n in (1, 2, 3, 4, 5, 6)] + [("ri", 0)]
                  + [("job", 7), ("job", 8), ("ri", 1), ("ada", 1)]
                  + [q_job(0), q_job(1), ("sn", 0), ("ri", 2), q_job(2), ("sn", 1), q_job(3), ("sn", 2), ("ri", 3)]
                  + [("ada", 2)]
                  + [q_job(4), ("sn", 3), q_job(5), ("sn", 4), q_job(6), ("sn", 5), q_job(7), ("sn", 6)]
                  + [("ada", 3)]
                  + [("job", 17), ("sn", 7)] + [("job", n) for n in (18, 19, 20)])
        JOBS0 = 21
        ORDER1 = ([("job", 0), ("ada", 5)] + [("job", 1), ("g1", 0)] + [("job", 2), ("job", 3), ("job", 4)]
                  + [("job", 5), ("g1", 1), ("job", 6), ("g1", 2), ("job", 7), ("g1", 3), ("job", 8)]
                  + [("job", n) for n in range(9, 25)])
        JOBS1 = 25

        def job_bank(n):
            return n % 4

        @block.scalar
        def _(act):
            act.dma_start(cT, A["c"].rearrange("a (p k) -> (a p) k", k=KT)).then_inc(s_c, 16)

            act.wait_ge(s_c, 16)
            act_.activation(cE, cT, ACT.Exp, scale=-1.0).then_inc(s_ce, 1)
            act.wait_ge(s_const, 1)

            def adaln_move(g):
                act.wait_ge(ada_mm, g)
                if g > 1:
                    act.wait_ge(ada_st, 16 * (g - 1))
                act_.activation(modrow, PS[:, 4, :], ACT.Copy).then_inc(ada_row, 1)

            def rms_from(dst, src, n):
                act_.activation(dst, src, ACT.Ln, scale=1.0 / n, bias=eps_c)
                act.drain()
                return act_.activation(dst, dst, ACT.Exp, scale=-0.5)

            def norm_stats(n, xbuf, t):
                layer, ffn = n // 2, n % 2
                if n == 0:
                    act.wait_ge(s_x[t], 16)
                elif ffn:
                    act.wait_ge(wo_x, 8 * layer + TT + t + 1)
                else:
                    act.wait_ge(s_comb, t + 1)
                act_.activation(xbuf[:, t, :], X[:, t, :], ACT.Square, accum_out=ssq[:, t:t + 1])
                act.drain()
                act_.activation(rstd[:, t:t + 1], ssq[:, t:t + 1], ACT.Sqrt, scale=1.0 / D, bias=eps_c)\
                    .then_inc(s_rstd, 1)

            def norm_move(n, t):
                if t == 0 and n:
                    act.wait_ge(s_ab, n + 1)
                act.wait_ge(nt_mm, TT * n + t + 1)
                ts_ = slice(t * P, (t + 1) * P)
                src = PS[:, 6, :].rearrange("p (k q) -> p k q", q=P)
                if n == 0:
                    act_.activation(hT[:, 0:4, ts_], src, ACT.Copy).then_inc(nt_a, 1)
                else:
                    for kt in range(4):
                        ins = act_.activation(hT[:, kt, ts_], src[:, kt, :], ACT.Identity,
                                              scale=Acol[n][:, kt:kt + 1], bias=Bcol[n][:, kt:kt + 1])
                    ins.then_inc(nt_a, 1)

            def ffn_norm(n, xbuf):
                norm_stats(n, xbuf, 0)
                for t in range(1, TT):
                    norm_stats(n, xbuf, t)
                    norm_move(n, t - 1)
                norm_move(n, TT - 1)

            def job0(n):
                act.wait_ge(job_mm, n + 1)
                src = PS[:, job_bank(n), :]
                if n == 0:
                    act_.activation(cumx[:, :], src, ACT.Identity, bias=fb).then_inc(job_out, 1)
                    act.drain()
                    act_.activation(rt, cumx[:, :], ACT.Abs)
                    act.drain()
                    act_.activation(rt, rt, ACT.Exp, scale=-1.0)
                    act.drain()
                    act_.activation(rt, rt, ACT.Ln, bias=1.0).then_inc(s_fl, 1)
                elif n < 5:
                    act_.activation(xr[:, n - 1, 3:3 + T], src, ACT.Copy).then_inc(job_out, 1)
                elif n < 9:
                    act_.activation(gate[:, n - 5, :], src, ACT.Copy).then_inc(job_out, 1)
                elif n < 17:
                    m = n - 9
                    if m >= 2:
                        act.wait_ge(sn_mm, m - 1)
                    act_.activation(sq[:, m % 2, :], src, ACT.Square).then_inc(s_sq, 1)
                    dst, gain = (qT, qg) if m < 4 else (kT, kg)
                    act_.activation(dst[:, m % 4, :], src, ACT.Identity, scale=gain).then_inc(job_out, 1)
                else:
                    if n == 17:
                        act.wait_ge(ri_mm, 4)
                    act_.activation(v_sb[:, n - 17, :], src, ACT.Copy).then_inc(job_out, 1)

            def head_norm(m):
                act.wait_ge(sn_mm, m + 1)
                if m >= 2:
                    act.wait_ge(s_qk, m - 1)
                rms_from(rstd_b[:, m % 2, :], PS[:, 5, :], HD).then_inc(s_rsb, 1)

            def rnn_gates(c):
                act.wait_ge(ri_mm, c + 1)
                if c:
                    act.wait_ge(s_yr, c)
                act_.activation(ri[:, 0, :], PS[:, 6, :], ACT.Sigmoid, bias=rb_c[:, c:c + 1])
                act_.activation(ri[:, 1, :], PS[:, 7, :], ACT.Sigmoid, bias=ib_c[:, c:c + 1]).then_inc(s_ri, 1)
                act.wait_ge(s_gz, c + 1)
                act_.activation(ru, ru, ACT.Sigmoid, scale=1.5957691216057308).then_inc(s_ge, 1)
                act.drain()
                act_.activation(ra, ri[:, 0, :], ACT.Exp, scale=nsp8[:, c:c + 1])
                act_.activation(rt, ri[:, 0, :], ACT.Tanh, scale=nsp8[:, c:c + 1]).then_inc(s_at, 1)
                act.wait_ge(s_v, c + 1)
                act_.activation(rt, rt, ACT.Sqrt).then_inc(s_sqv, 1)

            def lam_stage():
                act.wait_ge(s_lamE, 1)
                act_.activation(sp_t, sp_t, ACT.Exp, scale=-1.0).then_inc(s_lamx, 1)
                act.wait_ge(s_lamL, 1)
                act_.activation(nsp8, lw, ACT.Ln).then_inc(s_lamx, 1)

            for t in range(TT):
                norm_stats(0, xn, t)
                if t:
                    norm_move(0, t - 1)
            norm_move(0, TT - 1)
            for j in range(4):
                act.wait_ge(ada0_mm, j + 1)
                act_.activation(part0[j], PS[:, j, :], ACT.Copy).then_inc(s_part, 1)
            act.wait_ge(s_ab, 1)
            act.drain()
            for kt in range(4):
                act_.activation(hT[:, kt, :], hT[:, kt, :], ACT.Identity, scale=Acol[0][:, kt:kt + 1],
                                bias=Bcol[0][:, kt:kt + 1]).then_inc(s_h0, 1)
            act.wait_ge(s_prep, 1)
            for kind, i in ORDER0:
                if kind == "job":
                    job0(i)
                elif kind == "lam":
                    lam_stage()
                elif kind == "sn":
                    head_norm(i)
                elif kind == "ri":
                    rnn_gates(i)
                else:
                    adaln_move(i)

            def exps(n):
                h, t = head_tile(n)
                N = P * (t + 1)
                act.wait_ge(s_mx, n + 1)
                if n >= 2:
                    act.wait_ge(pt_mm, n - 1)
                act_.activation(prob[:, n % 2, 0:N], PS[:, n % 4, 0:N], ACT.Exp, bias=nmx[:, n % 4:n % 4 + 1],
                                accum_out=rsum[:, n % 4:n % 4 + 1]).then_inc(s_ex, 1)

            def move_pt(n):
                h, t = head_tile(n)
                act.wait_ge(pt_mm, n + 1)
                if h >= 2:
                    act.wait_ge(pv_mm, h // 2)
                act_.activation(pT[h % 2][:, 0:t + 1, t * P:(t + 1) * P],
                                PS[:, 4 + n % 2, 0:P * (t + 1)].rearrange("p (k q) -> p k q", q=P),
                                ACT.Copy).then_inc(s_pt, 1)
                if n % 8 == 7:
                    act.wait_ge(pv_mm, h // 2 + 1)
                    act_.activation(yfT[:, h // 2, :], PS[:, 6 + h // 2 % 2, :], ACT.Copy).then_inc(s_yf, 1)

            exps(0)
            for n in range(HEADS * TT):
                if n + 1 < HEADS * TT:
                    exps(n + 1)
                move_pt(n)
            ffn_norm(1, mxn[0])

            def moe(layer):
                b = layer * NE
                table(ACT.Sigmoid)
                act.wait_ge(z_mm, layer + 1)
                act_.activation(zT, PS[:, 7, :], ACT.Copy).then_inc(s_zt, 1)
                act.wait_ge(zt_mm, layer + 1)
                act_.activation(sc_r, PS[:, 6, 0:P].rearrange("p (t e) -> p t e", t=TT),
                                ACT.Sigmoid).then_inc(s_ez, 1)
                if layer == 0:
                    adaln_move(4)
                act.wait_ge(s_idx, layer + 1)

                def sigmoids(hx_, bank, hidden, expo):
                    act.wait_ge(*hidden)
                    act_.activation(hx_[:, 0:256], PS[:, bank, 0:256], ACT.Sigmoid).then_inc(expo, 1)

                def moves(hidT_, bank, transposed, moved, made, free, result, out):
                    act.wait_ge(*transposed)
                    act_.activation(hidT_, PS[:, 4, 0:256].rearrange("p (j s) -> p j s", j=2),
                                    ACT.Copy).then_inc(moved, 1)
                    act.wait_ge(*free)
                    settle(act, idle)
                    act.wait_ge(*made)
                    act_.activation(result, PS[:, bank, :], ACT.Copy).then_inc(out, 1)

                def further_moves(n):
                    moves(hidT_e, 7, (e_htm, n), e_ht, (e_ym, n), (e_st, n * 16), ysb_e, e_y)

                with act.Fori(0, NE // U) as it:
                    for u in range(U):
                        e = act.snap(it * U + u, min_val=0, max_val=NE - 1)
                        rounds = act.value_load(rounds_i[0:1, layer, ds(e, 1)], min_val=1, max_val=RMAX)
                        k = act.snap(it * U + (b + u + 1), min_val=1, max_val=2 * NE)
                        sigmoids(hx, 2, (h_mm, k), s_he)
                        with act.If(rounds > 1):
                            with act.If(rounds > 2):
                                with act.Fori(1, rounds - 1) as r:
                                    act.reg_add(extra_a, extra_a, 1)
                                    n = act.snap(extra_a, min_val=1, max_val=2 * NE * RMAX)
                                    sigmoids(hx_e, 3, (e_h, n), e_he)
                                    further_moves(n)
                                    act.drain()
                            act.reg_add(extra_a, extra_a, 1)
                            n = act.snap(extra_a, min_val=1, max_val=2 * NE * RMAX)
                            sigmoids(hx_e, 3, (e_h, n), e_he)
                        moves(hidT[:, u % 2, :, :], 5 + u % 2, (ht_mm, k), s_ht, (y_mm, k),
                              (y_st[u], it * 16 + 16 * (1 + layer * NE // U)), ysb[u], s_y)
                        with act.If(rounds > 1):
                            n = act.snap(extra_a, min_val=1, max_val=2 * NE * RMAX)
                            further_moves(n)
                            act.drain()
                        act.drain()

            def table(function):
                act.drain()
                act_.activation(idle_c, eps_c, function)

            def combine_tile(layer, t):
                act.wait_ge(y_in[t], 16 * (layer + 1))
                if t >= 2:
                    act.wait_ge(s_comb, layer * TT + t - 1)
                act_.activation(ct[t % 2], yk[t][:, 0, :], ACT.Identity,
                                scale=wk[:, 0, t:t + 1]).then_inc(s_y0, 1)

            extra_a = act.alloc_register("act_extra")
            act.reg_mov(extra_a, 0)
            idle = act.alloc_register("act_idle")
            act.reg_mov(idle, 0)
            moe(0)
            table(ACT.Sqrt)
            combine_tile(0, 0)
            combine_tile(0, 1)
            norm_stats(2, xn, 0)
            for t in range(TT):
                if t + 2 < TT:
                    combine_tile(0, t + 2)
                if t + 1 < TT:
                    norm_stats(2, xn, t + 1)
                norm_move(2, t)
            act.drain()


            def job1(n):
                act.wait_ge(job_mm, JOBS0 + n + 1)
                src = PS[:, job_bank(n), :]
                if n == 0:
                    act_.activation(glow, src[0:16, :], ACT.Copy).then_inc(job_out, 1)
                elif n < 9:
                    dst = q1 if n < 5 else k1
                    act_.activation(dst[:, (n - 1) % 4, :], src, ACT.Copy).then_inc(job_out, 1)
                elif n < 17:
                    half, t = divmod(n - 9, TT)
                    if n > 10:
                        act.wait_ge(s_silu, n - 10)
                    act_.activation(rexp[:, n % 2 * NC:(n % 2 + 1) * NC], src, ACT.Sigmoid)
                    act_.activation(r1[:, t, half * 512:half * 512 + 512], src, ACT.Copy).then_inc(job_out, 1)
                else:
                    half, t = divmod(n - 17, TT)
                    act_.activation(v1[:, t, half * 512:half * 512 + 512], src, ACT.Copy).then_inc(job_out, 1)

            def gates1(h):
                act.wait_ge(g1_mm, h + 1)
                if h:
                    act.wait_ge(s_kend, h)
                act_.activation(lg_t[:, 0, :], PS[:, 4 + h % 2, :], ACT.Identity, bias=gbias[:, h:h + 1])
                act.drain()
                act_.activation(lg_t[:, 1, :], lg_t[:, 0, :], ACT.Abs)
                act.drain()
                act_.activation(lg_t[:, 1, :], lg_t[:, 1, :], ACT.Exp, scale=-1.0)
                act.drain()
                act_.activation(lg_t[:, 1, :], lg_t[:, 1, :], ACT.Ln, bias=1.0).then_inc(s_g1l, 1)
                act.wait_ge(s_cm, h + 1)
                ends = cum1[:, h, :].rearrange("p (n c) -> p n c", c=CH)[:, :, CH - 1]
                act_.activation(lastc, ends, ACT.Copy)
                act_.activation(dec1[:, h, :], ends, ACT.Exp)
                act_.activation(lg_t[:, 0, :], cum1[:, h, :], ACT.Exp)
                act_.activation(lg_t[:, 1, :], cum1[:, h, :], ACT.Exp, scale=-1.0)
                act.drain()
                for n in range(NCH):
                    part = cum1[:, h, n * CH:(n + 1) * CH]
                    last = act_.activation(part, part, ACT.Exp, scale=-1.0, bias=lastc[:, n:n + 1])
                last.then_inc(s_ec, 1)

            for kind, i in ORDER1:
                if kind == "ada":
                    adaln_move(i)
                elif kind == "job":
                    job1(i)
                    if i == 5:
                        act.wait_ge(ada_st, 16 * 5)
                    if 5 <= i < 9:
                        gates1(i - 5)

            def keys_by_token(t):
                act.wait_ge(ke_mm, t + 1)
                for c in range(2):
                    rows = slice(c * CH, (c + 1) * CH)
                    ins = act_.activation(ketok[c][rows], PS[rows, 1, :].rearrange("p (h n) -> p h n", h=GH), ACT.Copy)
                ins.then_inc(s_ke, 1)

            keys_by_token(0)
            table(ACT.Sqrt)
            for t in range(TT):
                for h in range(GH):
                    act.wait_ge(o_mm, GH * t + h + 1)
                    act_.activation(PS[:, 2 + h, 256:512], PS[:, 2 + h, 0:256], ACT.Square,
                                    accum_out=o_ss[:, h:h + 1])
                act.drain()
                act_.activation(o_rs, o_ss, ACT.Sqrt, scale=1.0 / GDV, bias=eps_c).then_inc(s_ors, 1)
                if t + 1 < TT:
                    keys_by_token(t + 1)
                for half in range(2):
                    act.wait_ge(yt_mm, 2 * t + half + 1)
                    act_.activation(yT1[:, 4 * half:4 * half + 4, t * P:(t + 1) * P],
                                    PS[:, 6 + half, :].rearrange("p (k q) -> p k q", q=P), ACT.Copy).then_inc(s_yt, 1)
            ffn_norm(3, mxn[1])
            moe(1)
            for t in range(TT):
                combine_tile(1, t)
            for t in range(TT):
                act.wait_ge(s_comb, TT + t + 1)
                act.dma_start(out_v[:, t, :], X[:, t, :]).then_inc(s_out, 16)
            act.wait_ge(s_out, 16 * TT)

        @block.vector
        def _(dve):
            dve.wait_ge(s_ce, 1)
            vec.tensor_scalar(cE, cE, 1.0, None, ALU.add)
            dve.drain()
            vec.reciprocal(cE, cE)
            dve.drain()
            vec.tensor_tensor(cE, cE, cT, ALU.mult)
            dve.drain()
            vec.tensor_copy(keep_screp[:, :, :], cE.unsqueeze(2).broadcast_to([P, KT, 32])).then_inc(s_sc, 1)
            dve.wait_ge(s_const, 1)
            vec.tensor_reduce(sel_sum, ident[:, :].rearrange("p (g e) -> p e g", e=NE), X_AX, ALU.add)
            vec.tensor_reduce(sel4, ident[:, 0:P:32], X_AX, ALU.add).then_inc(s_sel4, 1)

            def columns(n):
                dve.wait_ge(s_mod, 32 * n)
                vec.scalar_tensor_tensor(out=Acol[n], in0=Acol[n], scalar=1.0, in1=gain_mf[n],
                                         op0=ALU.add, op1=ALU.mult).then_inc(s_ab, 1)

            def norm_rows(n, xbuf, t):
                dve.wait_ge(s_rstd, TT * n + t + 1)
                vec.reciprocal(rstd[:, t:t + 1], rstd[:, t:t + 1])
                dve.drain()
                vec.tensor_scalar(xbuf[:, t, :], X[:, t, :], rstd[:, t:t + 1], None, ALU.mult).then_inc(s_xn, 1)

            def norm_move(n, t):
                dve.wait_ge(nt_mm, TT * n + t + 1)
                src = PS[:, 7, :].rearrange("p (k q) -> p k q", q=P)
                dst = hT[:, 4:8, t * P:(t + 1) * P]
                if n == 0:
                    vec.tensor_copy(dst, src).then_inc(nt_v, 1)
                else:
                    vec.tensor_tensor(dst, src, Acol[n][:, 4:8].unsqueeze(2).broadcast_to([P, 4, P]), ALU.mult)
                    dve.drain()
                    vec.tensor_tensor(dst, dst, Bcol[n][:, 4:8].unsqueeze(2).broadcast_to([P, 4, P]), ALU.add)\
                        .then_inc(nt_v, 1)

            def lam_stage():
                dve.nop().then_inc(s_lamE, 1)
                dve.wait_ge(s_lamx, 1)
                vec.tensor_scalar(lw, sp_t, 1.0, None, ALU.add).then_inc(s_lamL, 1)
                dve.drain()
                vec.scalar_tensor_tensor(out=sp_t, in0=lw, scalar=-1.0, in1=sp_t, op0=ALU.add, op1=ALU.subtract)
                dve.wait_ge(s_lamx, 2)
                dve.drain()
                vec.reciprocal(lw, lw)
                dve.drain()
                vec.tensor_tensor(sp_t, sp_t, lw, ALU.mult)
                dve.drain()
                vec.tensor_tensor(nsp8, nsp8, sp_t, ALU.subtract)
                dve.drain()
                vec.tensor_scalar(sp_t, lamc, -1.0, 0.0, ALU.mult, ALU.max)
                dve.drain()
                vec.tensor_tensor(nsp8, nsp8, sp_t, ALU.add)
                dve.drain()
                vec.tensor_scalar(nsp8, nsp8, -RGLRU_C, None, ALU.mult)
                dve.drain()

            def one_over_one_plus(x):
                vec.tensor_scalar(x, x, 1.0, None, ALU.add)
                dve.drain()
                return vec.reciprocal(x, x)

            def rnn(c):
                dve.wait_ge(job_out, c + 2)
                vec.tensor_scalar(xc, xr[:, c, 3:3 + T], convw[:, 12 + c:13 + c], convb[:, c:c + 1],
                                  ALU.mult, ALU.add)
                dve.drain()
                for j in range(3):
                    ins = vec.scalar_tensor_tensor(out=xc, in0=xr[:, c, j:j + T], scalar=convw[:, 4 * j + c:4 * j + c + 1],
                                                   in1=xc, op0=ALU.mult, op1=ALU.add)
                    if j == 2:
                        ins.then_inc(s_xc, 1)
                    dve.drain()
                dve.wait_ge(job_out, c + 6)
                vec.tensor_tensor(ru, gate[:, c, :], gate[:, c, :], ALU.mult)
                dve.drain()
                vec.tensor_scalar(ru, ru, 0.044715, 1.0, ALU.mult, ALU.add)
                dve.drain()
                vec.tensor_tensor(ru, ru, gate[:, c, :], ALU.mult).then_inc(s_gz, 1)
                dve.wait_ge(s_ri, c + 1)
                dve.wait_ge(s_ge, c + 1)
                vec.tensor_tensor(gate[:, c, :], gate[:, c, :], ru, ALU.mult)
                vec.tensor_tensor(xc, xc, ri[:, 1, :], ALU.mult)
                dve.drain()
                dve.wait_ge(s_at, c + 1)
                vec.tensor_scalar(ru, rt, -1.0, 1.0, ALU.mult, ALU.add)
                dve.drain()
                vec.reciprocal(ru, ru)
                dve.drain()
                vec.scalar_tensor_tensor(out=rt, in0=rt, scalar=-2.0, in1=ru, op0=ALU.mult, op1=ALU.mult)\
                    .then_inc(s_v, 1)
                dve.wait_ge(s_sqv, c + 1)
                vec.tensor_tensor(xc, xc, rt, ALU.mult)
                dve.drain()
                vec.tensor_tensor_scan(rt, ra, xc, 0.0, ALU.mult, ALU.add)
                dve.drain()
                vec.tensor_tensor(xr[:, c, 3:3 + T], rt, gate[:, c, :], ALU.mult).then_inc(s_yr, 1)
                dve.drain()

            for t in range(TT):
                dve.wait_ge(s_x[t], 16)
                norm_rows(0, xn, t)
                if t:
                    norm_move(0, t - 1)
            norm_move(0, TT - 1)
            dve.wait_ge(s_small, 16 * N_SMALL)
            dve.wait_ge(col_mm, 1)
            vec.tensor_tensor(Bcol[0], Bcol[0], PS[:, 4, 0:KT], ALU.add)
            vec.scalar_tensor_tensor(out=Acol[0], in0=Acol[0], scalar=1.0, in1=PS[:, 4, KT:2 * KT],
                                     op0=ALU.add, op1=ALU.add)
            dve.drain()
            vec.tensor_tensor(Acol[0], Acol[0], gain_mf[0], ALU.mult).then_inc(s_ab, 1)
            dve.drain()
            for kt in range(4, KT):
                vec.tensor_scalar(hT[:, kt, :], hT[:, kt, :], Acol[0][:, kt:kt + 1], Bcol[0][:, kt:kt + 1],
                                  ALU.mult, ALU.add).then_inc(s_h0, 1)
            dve.wait_ge(pr_mm, 1)
            vec.tensor_copy(pcols, PS[:, 5, 0:NPC])
            dve.drain()
            vec.scalar_tensor_tensor(out=sp_t, in0=lamc, scalar=-1.0, in1=lamc, op0=ALU.mult, op1=ALU.max)
            vec.tensor_scalar(qg, qg, HD ** -0.5, None, ALU.mult).then_inc(s_prep, 1)
            dve.drain()
            lam_stage()
            dve.wait_ge(s_fl, 1)
            vec.scalar_tensor_tensor(out=cumx[:, :], in0=cumx[:, :], scalar=0.0, in1=rt, op0=ALU.min, op1=ALU.subtract)
            vec.memset(ru, 1.0)
            dve.drain()
            vec.tensor_tensor_scan(cumx[:, :], ru, cumx[:, :], 0.0, ALU.mult, ALU.add).then_inc(s_cum, 1)
            dve.drain()
            for c in range(4):
                rnn(c)

            def row_max(n):
                h, t = head_tile(n)
                dve.wait_ge(sc_mm, n + 1)
                diag = PS[:, n % 4, t * P:(t + 1) * P]
                vec.tensor_tensor(diag, diag, maskneg[:, :], ALU.add)
                dve.drain()
                vec.tensor_reduce(nmx[:, n % 4:n % 4 + 1], PS[:, n % 4, 0:P * (t + 1)], X_AX, ALU.max,
                                  negate=True).then_inc(s_mx, 1)

            dve.wait_ge(s_qk, 8)
            dve.wait_ge(s_rsb, 8)
            dve.wait_ge(ada_st, 16 * 3)
            for par in range(2):
                for hh in range(2):
                    own, other = slice(HD * hh, HD * hh + HD), slice(HD - HD * hh, P - HD * hh)
                    if par == 0:
                        vec.tensor_copy(kz[hh][own, 0, :], kT[own, 0, :])
                    ins = vec.tensor_copy(kz[hh][other, par, :], cumx[other, :])
                ins.then_inc(s_kz0, 1)

            row_max(0)
            for n in range(HEADS * TT):
                if n + 1 < HEADS * TT:
                    row_max(n + 1)
                N = P * (n // 2 % TT + 1)
                dve.wait_ge(s_ex, n + 1)
                vec.reciprocal(rinv[:, n % 4:n % 4 + 1], rsum[:, n % 4:n % 4 + 1])
                dve.drain()
                vec.tensor_scalar(prob[:, n % 2, 0:N], prob[:, n % 2, 0:N], rinv[:, n % 4:n % 4 + 1], None,
                                  ALU.mult).then_inc(s_pn, 1)

            def add_output(layer, bank0):
                n, xbuf = 2 * layer + 1, mxn[layer]
                dve.wait_ge(s_gB, 16 * (2 * layer + 1))
                columns(n)
                for o in range(8):
                    half, t = divmod(o, TT)
                    cs = slice(half * NC, (half + 1) * NC)
                    dve.wait_ge(wo_mm, 8 * layer + o + 1)
                    vec.tensor_tensor(out_tmp, PS[:, bank0 + o % 4, :], gB[:, cs], ALU.mult)
                    dve.drain()
                    vec.tensor_tensor(X[:, t, cs], X[:, t, cs], out_tmp, ALU.add).then_inc(wo_x, 1)
                    dve.drain()
                    if half:
                        norm_rows(n, xbuf, t)
                        if t:
                            norm_move(n, t - 1)
                norm_move(n, TT - 1)

            def bc(ap, *shape):
                return ap.broadcast_to([P, *shape])

            def pick(O):
                vec.tensor_reduce(gm_r, sel_r, X_AX, ALU.max)
                dve.drain()
                vec.tensor_tensor(O, sel_r, bc(gm_r.unsqueeze(2), TT, NE), ALU.is_ge)
                dve.drain()
                vec.tensor_tensor(O, O, bc(wE.unsqueeze(1), TT, NE), ALU.mult)
                dve.drain()
                vec.tensor_reduce(gm_r, O, X_AX, ALU.max)
                dve.drain()
                vec.tensor_tensor(O, O, bc(gm_r.unsqueeze(2), TT, NE), ALU.is_equal)
                dve.drain()

            def router(layer):
                dve.wait_ge(s_const, 3 if layer == 0 else 4)
                dve.wait_ge(s_ez, layer + 1)
                vec.tensor_tensor(sel_r, sc_r, bc(rbB.unsqueeze(1), TT, NE), ALU.add)
                dve.drain()
                for i in range(TT * NG):
                    t, g = divmod(i, NG)
                    vec.max(top8[:, i, :], sel_r[:, t, g * EG:(g + 1) * EG])
                dve.drain()
                vec.tensor_tensor(gs_r.rearrange("p t g -> p (t g)"), top8[:, :, 0], top8[:, :, 1], ALU.add)
                dve.drain()
                vec.tensor_reduce(gm_r, gs_r, X_AX, ALU.max)
                dve.drain()
                vec.tensor_tensor(gv_r, gs_r, bc(gm_r.unsqueeze(2), TT, NG), ALU.is_ge)
                dve.drain()
                vec.tensor_tensor(gv_r, gv_r, bc(wG.unsqueeze(1), TT, NG), ALU.mult)
                dve.drain()
                vec.tensor_reduce(gm_r, gv_r, X_AX, ALU.max)
                dve.drain()
                vec.tensor_tensor(gv_r, gv_r, bc(gm_r.unsqueeze(2), TT, NG), ALU.is_equal)
                dve.drain()
                flat = sel_r.rearrange("p t (g x) -> p (t g) x", g=NG)
                gvf = gv_r.rearrange("p t g -> p (t g)")
                vec.tensor_scalar(gs_r, gv_r, 1e30, -1e30, ALU.mult, ALU.add)
                vec.tensor_tensor(flat, flat, bc(gvf.unsqueeze(2), TT * NG, EG), ALU.mult)
                dve.drain()
                vec.tensor_tensor(flat, flat,
                                  bc(gs_r.rearrange("p t g -> p (t g)").unsqueeze(2), TT * NG, EG), ALU.add)
                dve.drain()
                pick(O1)
                vec.scalar_tensor_tensor(out=sel_r, in0=O1, scalar=-1e30, in1=sel_r, op0=ALU.mult, op1=ALU.add)
                dve.drain()
                pick(O2)
                vec.tensor_tensor(hot_b, O1, O2, ALU.add).then_inc(s_hot, 1)
                for k, O in enumerate((O1, O2)):
                    vec.tensor_tensor(tmp_r, O, sc_r, ALU.mult)
                    dve.drain()
                    vec.tensor_reduce(wk[:, k, :], tmp_r, X_AX, ALU.add)
                    dve.drain()
                vec.tensor_tensor(gm_r, wk[:, 0, :], wk[:, 1, :], ALU.add)
                dve.drain()
                vec.reciprocal(gm_r, gm_r)
                dve.drain()
                vec.tensor_tensor(wk, wk, bc(gm_r.unsqueeze(1), 2, TT), ALU.mult)
                dve.wait_ge(pos_mm, layer + 1)
                pos = PS[:, 0, 0:TT * NE].rearrange("p (t e) -> p t e", t=TT)
                for k, O in enumerate((O1, O2)):
                    vec.tensor_tensor(tmp_r, O, pos, ALU.mult)
                    dve.drain()
                    vec.tensor_reduce(posk[:, k, :], tmp_r, X_AX, ALU.add)
                    dve.drain()
                pk = posk.rearrange("p k t -> p (k t)")
                vec.tensor_tensor(ge, bc(pk.unsqueeze(2), 2 * TT, 9), bc(thr.unsqueeze(1), 2 * TT, 9), ALU.is_ge)
                dve.drain()
                qf = qm.rearrange("p k t -> p (k t)")
                vec.tensor_reduce(qf, ge[:, :, 1:9], X_AX, ALU.add)
                vec.tensor_tensor(rvv, ge[:, :, 0:8], ge[:, :, 1:9], ALU.subtract)
                dve.drain()
                vec.scalar_tensor_tensor(out=qf, in0=qf, scalar=-float(SL), in1=pk, op0=ALU.mult, op1=ALU.add)
                vec.tensor_tensor(rvv, rvv, bc(tokv.rearrange("p k t -> p (k t)").unsqueeze(2), 2 * TT, 8), ALU.mult)
                dve.drain()
                vec.tensor_tensor(Aoh, bc(io64.unsqueeze(1), 2 * TT, P), bc(qf.unsqueeze(2), 2 * TT, P), ALU.is_equal)
                for k, O in enumerate((O1, O2)):
                    for t in range(TT):
                        ins = vec.tensor_tensor(Boh[:, k, t, :].rearrange("p (e r) -> p e r", r=8),
                                                bc(O[:, t, :].unsqueeze(2), NE, 8),
                                                bc(rvv[:, TT * k + t, :].unsqueeze(1), NE, 8), ALU.mult)
                ins.then_inc(s_tab, 1)
                vec.tensor_copy(cnt_f, PS[0:1, 1, 0:NE])
                dve.drain()
                over = tabf[0:1, 0:NE * (RMAX - 1)].rearrange("p (e r) -> p e r", e=NE)
                vec.tensor_tensor(over, cnt_f.unsqueeze(2).broadcast_to([1, NE, RMAX - 1]),
                                  thr[0:1, 1:RMAX].unsqueeze(1).broadcast_to([1, NE, RMAX - 1]), ALU.is_gt)
                dve.drain()
                vec.tensor_reduce(rnd_f, over, X_AX, ALU.add)
                dve.drain()
                vec.tensor_scalar(rounds_i[0:1, layer, 0:NE], rnd_f, 1.0, None, ALU.add)
                vec.memset(rounds_i[0:1, layer, NE:NE + U], 1)
                dve.wait_ge(tab_mm, layer + 1)
                raw = PS[:, 4, 0:NE * 8]
                vec.tensor_scalar(tabf, raw, -0.5, p4p, ALU.is_ge, ALU.mult)
                vec.memset(idx_i[:, NE * 8:NIDX], int(BIG))
                dve.drain()
                vec.scalar_tensor_tensor(out=idx_i[:, 0:NE * 8], in0=raw, scalar=c1p, in1=tabf,
                                         op0=ALU.add, op1=ALU.add)
                dve.drain()
                vec.tensor_scalar(gidx_i, idx_i, 2, None, ALU.logical_shift_right)
                dve.drain()
                for u in range(U):
                    vec.tensor_copy(gcur[u], gidx_i[:, u * 8:u * 8 + 1])
                    ins = vec.tensor_copy(ghi[u], gidx_i[:, u * 8 + 1:u * 8 + 2])
                ins.then_inc(s_idx, 1)
                dve.drain()

            def modulate(n_norm, rows_T, bank, rows, mod):
                dve.wait_ge(*rows)
                src = PS[:, bank, :].rearrange("p (k s) -> p k s", k=KT)
                vec.tensor_tensor(rows_T, src, bc(Acol[n_norm].unsqueeze(2), KT, SL), ALU.mult)
                dve.drain()
                vec.tensor_tensor(rows_T, rows_T, bc(Bcol[n_norm].unsqueeze(2), KT, SL), ALU.add).then_inc(mod, 1)

            def activate(hx_, hidb_, bank, expo, hidden):
                dve.wait_ge(*expo)
                h1, h3 = PS[:, bank, 0:256], PS[:, bank, 256:512]
                vec.tensor_tensor(hx_[:, 256:512], hx_[:, 0:256], h1, ALU.mult)
                dve.drain()
                vec.tensor_tensor(hidb_, hx_[:, 256:512], h3, ALU.mult).then_inc(hidden, 1)

            def moe(layer):
                b = layer * NE
                n_norm = 2 * layer + 1
                router(layer)

                def further_rows(n, column):
                    modulate(n_norm, xgT_e, 7, (e_xt, n), e_sxt)
                    dve.wait_ge(e_st, n * 16)
                    settle(dve, idle)
                    vec.tensor_copy(icur_e, idx_i[:, ds(column, 1)])

                def further_hidden(n):
                    activate(hx_e, hidb_e, 3, (e_he, n), e_hid)

                with dve.Fori(0, NE // U) as it:
                    for u in range(U):
                        e = dve.snap(it * U + u, min_val=0, max_val=NE - 1)
                        rounds = dve.value_load(rounds_i[0:1, layer, ds(e, 1)], min_val=1, max_val=RMAX)
                        k = dve.snap(it * U + (b + u + 1), min_val=1, max_val=2 * NE)
                        c = dve.snap(e * 8, min_val=0, max_val=(NE - 1) * 8)
                        vec.tensor_copy(gcur_e, gidx_i[:, ds(c + 2, 1)]).then_inc(s_ecur, 1)
                        modulate(n_norm, xgT[:, u % 2], u % 2, (xt_mm, it * U + (layer * (NE + 1) + u + 1)), s_xt)
                        dve.wait_ge(y_st[u], it * 16 + 16 * (1 + layer * NE // U))
                        settle(dve, idle)
                        vec.tensor_copy(icur[u], idx_i[:, ds(c, 1)])
                        vec.tensor_copy(gcur[u], gidx_i[:, ds(c + 8 * U, 1)])
                        with dve.If(rounds > 1):
                            with dve.If(rounds > 2):
                                with dve.Fori(2, rounds) as r:
                                    dve.reg_add(extra, extra, 1)
                                    n = dve.snap(extra, min_val=1, max_val=2 * NE * RMAX)
                                    further_rows(n, c + r)
                                    further_hidden(n)
                                    vec.tensor_copy(gcur_e, gidx_i[:, ds(c + r + 1, 1)]).then_inc(s_ecur, 1)
                                    dve.drain()
                            dve.reg_add(extra, extra, 1)
                            n = dve.snap(extra, min_val=1, max_val=2 * NE * RMAX)
                            further_rows(n, c + 1)
                        vec.tensor_copy(ghi[u], gidx_i[:, ds(c + 8 * U + 1, 1)])
                        activate(hx, hidb[:, u % 2, :], 2, (s_he, k), s_hid)
                        with dve.If(rounds > 1):
                            n = dve.snap(extra, min_val=1, max_val=2 * NE * RMAX)
                            further_hidden(n)
                            dve.drain()
                        dve.drain()

            def combine_tile(layer, t):
                if t == 0:
                    dve.wait_ge(s_gB, 16 * (2 * layer + 2))
                c = ct[t % 2]
                dve.wait_ge(s_y0, layer * TT + t + 1)
                vec.scalar_tensor_tensor(out=c, in0=yk[t][:, 1, :], scalar=wk[:, 1, t:t + 1], in1=c,
                                         op0=ALU.mult, op1=ALU.add)
                dve.drain()
                vec.tensor_tensor(c, c, gB[:, :], ALU.mult)
                dve.drain()
                vec.tensor_tensor(X[:, t, :], X[:, t, :], c, ALU.add).then_inc(s_comb, 1)
                dve.drain()

            extra = dve.alloc_register("dve_extra")
            dve.reg_mov(extra, 0)
            idle = dve.alloc_register("dve_idle")
            dve.reg_mov(idle, 0)
            add_output(0, 0)
            moe(0)
            columns(2)
            combine_tile(0, 0)
            combine_tile(0, 1)
            norm_rows(2, xn, 0)
            for t in range(TT):
                if t + 2 < TT:
                    combine_tile(0, t + 2)
                if t + 1 < TT:
                    norm_rows(2, xn, t + 1)
                norm_move(2, t)
            dve.drain()

            dve.wait_ge(s_const, 3)
            for h in range(GH):
                dve.wait_ge(s_g1l, h + 1)
                g = lg_t[:, 0, :]
                vec.scalar_tensor_tensor(out=g, in0=g, scalar=0.0, in1=lg_t[:, 1, :], op0=ALU.min, op1=ALU.subtract)
                dve.drain()
                vec.tensor_scalar(g, g, 1.0 / GATE_TAU, None, ALU.mult)
                dve.drain()
                vec.tensor_tensor_scan(cum1[:, h, :], cmask[:, :], g, 0.0, ALU.mult, ALU.add).then_inc(s_cm, 1)
                dve.wait_ge(s_ec, h + 1)
                vec.scalar_tensor_tensor(out=q1[:, h, :], in0=q1[:, h, :], scalar=GDK ** -0.5, in1=lg_t[:, 0, :],
                                         op0=ALU.mult, op1=ALU.mult)
                vec.tensor_tensor(kend[:, h, :], k1[:, h, :], cum1[:, h, :], ALU.mult)
                dve.drain()
                vec.tensor_tensor(k1[:, h, :], k1[:, h, :], lg_t[:, 1, :], ALU.mult).then_inc(s_kend, 1)
                dve.drain()
            vec.memset(state, 0.0)
            for c in range(2):
                other = slice((1 - c) * CH, (2 - c) * CH)
                ins = vec.memset(ketok[c][other], 0.0)
            ins.then_inc(s_kz, 1)
            dve.drain()

            for n in range(9, 17):
                half, t = divmod(n - 9, TT)
                dve.wait_ge(job_out, JOBS0 + n + 1)
                part = r1[:, t, half * NC:(half + 1) * NC]
                vec.tensor_tensor(part, part, rexp[:, n % 2 * NC:(n % 2 + 1) * NC], ALU.mult).then_inc(s_silu, 1)
                if n == 9:
                    dve.wait_ge(s_small1, 48)
                dve.drain()
                two = part.rearrange("p (h n) -> p h n", n=GDV)
                vec.tensor_tensor(two, two, bc(ogain.unsqueeze(1), 2, GDV), ALU.mult)
            dve.drain()

            def update_state(t, h, c):
                dve.wait_ge(oi_mm if c == 0 else o_mm, GH * t + h + 1)
                kv = PS[:, (6, 0)[c] + h // 2, (h % 2) * GDV:(h % 2 + 1) * GDV]
                vec.scalar_tensor_tensor(out=state[:, h, :], in0=state[:, h, :],
                                         scalar=dec1[:, h, 2 * t + c:2 * t + c + 1], in1=kv,
                                         op0=ALU.mult, op1=ALU.add).then_inc(s_st, 1)

            def masked(t):
                dve.wait_ge(it_mm, t + 1)
                vec.tensor_tensor(itm, PS[:, 0, :].rearrange("p (h n) -> p h n", h=GH),
                                  bc(tri1[:, :].unsqueeze(1), GH, P), ALU.mult).then_inc(s_it, 1)

            masked(0)
            for t in range(TT):
                for c in range(2):
                    dve.drain()
                    for h in range(GH):
                        update_state(t, h, c)
                if t + 1 < TT:
                    masked(t + 1)
                dve.wait_ge(s_ors, t + 1)
                vec.reciprocal(o_rs, o_rs)
                dve.drain()
                for h in range(GH):
                    y = r1[:, t, h * GDV:(h + 1) * GDV]
                    ins = vec.scalar_tensor_tensor(out=y, in0=PS[:, 2 + h, 0:GDV], scalar=o_rs[:, h:h + 1], in1=y,
                                                   op0=ALU.mult, op1=ALU.mult)
                ins.then_inc(s_yo, 1)
            add_output(1, 2)
            moe(1)
            for t in range(TT):
                combine_tile(1, t)

        @block.tensor
        def _(pe):
            def mm(out, lhsT, rhs, first, last):
                return ten.matmul(out, lhsT, rhs, start=first, stop=last)

            def used(n=1):
                pe.drain()
                for _ in range(n):
                    ten.nop().then_inc(piece_used, 1)

            def adaln(g):
                if g > 1:
                    pe.wait_ge(ada_row, g - 1)
                for j in range(4):
                    landed(pe, ADA[g] + j)
                for kt in range(KT):
                    for j in range(4):
                        ins = mm(PS[32 * j:32 * j + 32, 4, :], keep_screp[:, kt, :], piece_ap(ADA[g] + j)[:, kt, :],
                                 kt == 0, kt == KT - 1)
                ins.then_inc(ada_mm, 1)
                used(4)

            def adaln_first():
                for j in range(4):
                    landed(pe, ADA[0] + j)
                    for i in range(2):
                        for g in range(4):
                            kt = g + 4 * i
                            ins = mm(PS[32 * g:32 * g + 32, j, :], keep_screp[:, kt, :],
                                     piece_ap(ADA[0] + j)[:, kt, :], i == 0, i == 1)
                    ins.then_inc(ada0_mm, 1)
                    used()
                pe.wait_ge(s_sel4, 1)
                for j in range(4):
                    pe.wait_ge(s_part, j + 1)
                    c, w = j % 2, j // 2
                    for kt in range(KT):
                        ins = mm(PS[64 * c:64 * c + 64, 4, w * KT + kt:w * KT + kt + 1],
                                 part0[j].rearrange("p (q k) -> p k q", k=KT)[:, kt, :], sel4, True, True)
                ins.then_inc(col_mm, 1)

            def norm_transposes(n, xbuf, t):
                pe.wait_ge(s_xn, TT * n + t + 1)
                if t:
                    pe.wait_ge(nt_a, TT * n + t)
                    pe.wait_ge(nt_v, TT * n + t)
                for kt in range(KT):
                    src = xbuf[:, t, :].rearrange("p (q k) -> p k q", k=KT)[:, kt, :]
                    ins = ten.transpose(PS[:, 6 + kt // 4, kt % 4 * P:(kt % 4 + 1) * P], src, ident[:, :])
                ins.then_inc(nt_mm, 1)

            def norm_complete(n):
                pe.wait_ge(nt_a, TT * (n + 1))
                pe.wait_ge(nt_v, TT * (n + 1))

            def job0(n):
                if n >= 4:
                    pe.wait_ge(job_out, n - 3)
                out = PS[:, job_bank(n), :]
                if n:
                    piece, ct_ = WIN0[(n - 1) // 4], (n - 1) % 4
                    landed(pe, piece)
                for kt in range(KT):
                    if n == 0:
                        lhsT, rhs = wfx[:, kt, :], hT[:, kt, :]
                    elif n < 17:
                        lhsT, rhs = piece_ap(piece)[:, kt, ct_ * P:(ct_ + 1) * P], hT[:, kt, :]
                    else:
                        lhsT, rhs = hT[:, kt, ct_ * P:(ct_ + 1) * P], piece_ap(piece)[:, kt, :]
                    ins = mm(out, lhsT, rhs, kt == 0, kt == KT - 1)
                ins.then_inc(job_mm, 1)
                if n and ct_ == 3:
                    used()

            pe.wait_ge(s_const, 1)
            pe.wait_ge(s_sc, 1)
            for t in range(TT):
                norm_transposes(0, xn, t)
            adaln_first()
            pe.wait_ge(s_pr, 16 * 12)
            ten.transpose(PS[:, 5, 0:NPC], prow, ident[0:NPC, 0:NPC]).then_inc(pr_mm, 1)
            pe.wait_ge(s_h0, KT)
            pe.wait_ge(s_fx, 16 * 6)
            for kind, i in ORDER0:
                if kind == "job":
                    job0(i)
                elif kind == "ada":
                    adaln(i)
                elif kind == "ri":
                    pe.wait_ge(s_xc, i + 1)
                    if i:
                        pe.wait_ge(s_ri, i)
                    mm(PS[:, 6, :], bd[:, 0, i, :], xc, True, True)
                    mm(PS[:, 7, :], bd[:, 1, i, :], xc, True, True).then_inc(ri_mm, 1)
                elif kind == "sn":
                    pe.wait_ge(s_sq, i + 1)
                    if i:
                        pe.wait_ge(s_rsb, i)
                    mm(PS[:, 5, :], blk64[:, :], sq[:, i % 2, :], True, True).then_inc(sn_mm, 1)

            def scores(m):
                if m >= 2:
                    pe.wait_ge(s_ex, 2 * m - 2)
                for n in (2 * m, 2 * m + 1):
                    h, t = head_tile(n)
                    N = P * (t + 1)
                    out = PS[:, n % 4, 0:N]
                    pe.wait_ge(s_qz, n + 1)
                    pe.wait_ge(s_kz0, 1 + (h >= 2))
                    mm(out, qz[:, n % 2, m % 2, :], kz[h % 2][:, h // 2 % 2, 0:N], True, True).then_inc(sc_mm, 1)

            pe.wait_ge(job_out, JOBS0)
            pe.wait_ge(s_cum, 1)
            pe.wait_ge(s_qk, 8)
            pe.wait_ge(s_rsb, 8)
            pe.wait_ge(ada_row, 4 - 1)
            scores(0)
            for n in range(HEADS * TT):
                h, t = head_tile(n)
                if n % 2 == 0 and n + 2 < HEADS * TT:
                    scores(n // 2 + 1)
                pe.wait_ge(s_pn, n + 1)
                if n >= 2:
                    pe.wait_ge(s_pt, n - 1)
                for kb in range(t + 1):
                    ins = ten.transpose(PS[:, 4 + n % 2, kb * P:(kb + 1) * P], prob[:, n % 2, kb * P:(kb + 1) * P],
                                        ident[:, :])
                ins.then_inc(pt_mm, 1)
                if n % 8 == 7:
                    pr = h // 2
                    pe.wait_ge(s_pt, n + 1)
                    if pr >= 2:
                        pe.wait_ge(s_yf, pr - 1)
                    for kb in range(TT):
                        for hh in range(2):
                            hd = 2 * pr + hh
                            ins = mm(PS[64 * hh:64 * hh + 64, 6 + pr % 2, kb * P:T],
                                     v_sb[:, kb, hd * HD:(hd + 1) * HD], pT[hh][:, kb, kb * P:T],
                                     kb == 0, kb == TT - 1)
                    ins.then_inc(pv_mm, 1)

            def output_projection(layer, bank0, first, lhs):
                for o in range(8):
                    half, t = divmod(o, TT)
                    if o == 0 or o == TT:
                        landed(pe, first[half])
                    if o >= 4:
                        pe.wait_ge(wo_x, 8 * layer + o - 3)
                    for kt in range(KT):
                        ins = mm(PS[:, bank0 + o % 4, :], lhs(kt, t), piece_ap(first[half])[:, kt, :],
                                 kt == 0, kt == KT - 1)
                    ins.then_inc(wo_mm, 1)
                    if t == TT - 1:
                        used()
                    if o > TT:
                        norm_transposes(2 * layer + 1, mxn[layer], t - 1)
                norm_transposes(2 * layer + 1, mxn[layer], TT - 1)
                norm_complete(2 * layer + 1)

            pe.wait_ge(s_yr, 4)
            pe.wait_ge(s_yf, 4)
            output_projection(0, 0, WOUT0, lambda kt, t: (
                xr[:, kt, 3 + t * P:3 + (t + 1) * P] if kt < 4 else yfT[:, kt - 4, t * P:(t + 1) * P]))

            def transpose_rows(bank, source, rows, xt, base=0):
                slots = slice(base, base + SL)
                pe.wait_ge(*rows)
                ten.matmul(PS[:, bank, 0:1], ident[slots, :], ident[slots, 0:1], start=True, stop=True)
                for kt in range(KT):
                    src = source.rearrange("p (q k) -> p k q", k=KT)[:, kt, :]
                    ins = ten.transpose(PS[:, bank, kt * SL:(kt + 1) * SL], src, ident[slots, slots])
                ins.then_inc(xt, 1)

            def hidden_products(slot, rows_T, bank, mod, hm, weights):
                w13 = ring[:, slot:slot + 2, :].rearrange("p w (k f) -> p w k f", k=KT)
                pe.wait_ge(*mod)
                weights(0)
                for kt in range(KT):
                    for half in range(2):
                        ins = mm(PS[SL * half:SL * half + SL, bank, :].rearrange("p (w f) -> p w f", w=2),
                                 rows_T[:, kt, :], w13[:, :, kt, half * 256:(half + 1) * 256],
                                 kt == 0, kt == KT - 1)
                ins.then_inc(hm, 1)

            def output_products(slot, hidb_, hidT_, bank, hidden, htm, moved, ym, weights):
                w2 = ring[:, (slot + 2) % SLOTS, :].rearrange("p (h j n) -> p h j n", h=2, j=2)
                pe.wait_ge(*hidden)
                for j in range(2):
                    ins = ten.transpose(PS[:, 4, j * P:(j + 1) * P],
                                        hidb_.rearrange("p (q j) -> p j q", j=2)[:, j, :], ident[:, :])
                ins.then_inc(htm, 1)
                pe.wait_ge(*moved)
                weights(1)
                for i in range(4):
                    h, j = divmod(i, 2)
                    for half in range(2):
                        ins = mm(PS[SL * half:SL * half + SL, bank, :], hidT_[:, j, h * SL:(h + 1) * SL],
                                 w2[:, h, j, half * NC:(half + 1) * NC], i == 0, i == 3)
                ins.then_inc(ym, 1)

            def moe(layer, first):
                b = layer * NE
                before = layer * (NE + U) // U
                for i in range(2):
                    for g in range(4):
                        kt = g + 4 * i
                        ins = mm(PS[NE * g:NE * (g + 1), 7, :], rw_sb[:, kt, :], hT[:, kt, :], i == 0, i == 1)
                ins.then_inc(z_mm, 1)
                pe.wait_ge(s_zt, layer + 1)
                for t in range(TT):
                    ins = mm(PS[:, 6, t * NE:(t + 1) * NE], zT[:, t * P:(t + 1) * P], sel_sum, True, True)
                ins.then_inc(zt_mm, 1)
                if layer == 0:
                    adaln(4)
                pe.wait_ge(s_hot, layer + 1)
                for t in range(TT):
                    for tp in range(t + 1):
                        mm(PS[:, 0, t * NE:(t + 1) * NE], triS if tp == t else ones_b, hot_b[:, tp, :],
                           tp == 0, tp == t)
                for t in range(TT):
                    ins = mm(PS[:, 1, 0:NE], ones_b, hot_b[:, t, :], t == 0, t == TT - 1)
                ins.then_inc(pos_mm, 1)
                pe.wait_ge(s_tab, layer + 1)
                if layer == 0:
                    pe.wait_ge(ada_row, 4)
                for i in range(2 * TT):
                    ins = mm(PS[:, 4, 0:NE * 8], Aoh[:, i, :], Boh[:, i // TT, i % TT, :], i == 0, i == 2 * TT - 1)
                ins.then_inc(tab_mm, 1)
                pe.wait_ge(s_idx, layer + 1)
                transpose_rows(0, xg[0:SL, 0, :], (g_in[0], 16 * (before + 1)), xt_mm)
                with pe.Fori(0, NE // U) as it:
                    for u in range(U):
                        e = pe.snap(it * U + u, min_val=0, max_val=NE - 1)
                        rounds = pe.value_load(rounds_i[0:1, layer, ds(e, 1)], min_val=1, max_val=RMAX)
                        k = pe.snap(it * U + (b + u + 1), min_val=1, max_val=2 * NE)
                        piece = first + 3 * u

                        def weights(part):
                            for p in ((piece, piece + 1), (piece + 2,))[part]:
                                pe.wait_ge(slot_in[slot_of(p)], it * (16 * 3 * U // SLOTS) + 16 * (p // SLOTS + 1))
                        slot, rows_u, hid_u = slot_of(piece), xgT[:, u % 2], hidb[:, u % 2, :]

                        def further_hidden(n, own):
                            if own:
                                pe.wait_ge(e_y, n)
                                settle(pe, idle)
                                transpose_rows(7, xg_e, own, e_xt)
                            else:
                                pe.wait_ge(e_y, n)
                                settle(pe, idle)
                                pe.reg_add(hi[u], hi[u], 1)
                                g = pe.snap(hi[u], min_val=1, max_val=2 * NE)
                                transpose_rows(7, xg[SL:P, u, :], (g_hi[u], g * 16), e_xt, base=SL)
                            hidden_products(slot, xgT_e, 3, (e_sxt, n), e_h, weights)

                        def further_output(n):
                            output_products(slot, hidb_e, hidT_e, 7, (e_hid, n), e_htm, (e_ht, n), e_ym, weights)

                        hidden_products(slot, rows_u, 2, (s_xt, k), h_mm, weights)
                        v = (u + 1) % U
                        transpose_rows(v % 2, xg[0:SL, v, :], (g_in[v], it * 16 + 16 * (before + 1 + (u + 1) // U)),
                                       xt_mm)
                        with pe.If(rounds > 1):
                            with pe.If(rounds > 2):
                                with pe.Fori(1, rounds - 1) as r:
                                    pe.reg_add(extra, extra, 1)
                                    pe.reg_add(deep, deep, 1)
                                    n = pe.snap(extra, min_val=1, max_val=2 * NE * RMAX)
                                    d = pe.snap(deep, min_val=1, max_val=2 * NE * RMAX)
                                    further_hidden(n, (e_g, d * 16))
                                    further_output(n)
                                    pe.drain()
                            pe.reg_add(extra, extra, 1)
                            n = pe.snap(extra, min_val=1, max_val=2 * NE * RMAX)
                            further_hidden(n, None)
                            pe.drain()
                        used(2)
                        output_products(slot, hid_u, hidT[:, u % 2], 5 + u % 2, (s_hid, k), ht_mm, (s_ht, k), y_mm,
                                        weights)
                        with pe.If(rounds > 1):
                            n = pe.snap(extra, min_val=1, max_val=2 * NE * RMAX)
                            further_output(n)
                            pe.drain()
                        used(1)

            extra = pe.alloc_register("pe_extra")
            pe.reg_mov(extra, 0)
            hi = [pe.alloc_register(f"pe_hi{u}") for u in range(U)]
            for reg in hi:
                pe.reg_mov(reg, 0)
            deep = pe.alloc_register("pe_deep")
            pe.reg_mov(deep, 0)
            idle = pe.alloc_register("pe_idle")
            pe.reg_mov(idle, 0)
            moe(0, MOE0)

            for t in range(TT):
                norm_transposes(2, xn, t)
            norm_complete(2)
            pe.wait_ge(s_small1, 32)
            for kind, i in ORDER1:
                if kind == "ada":
                    adaln(i)
                    continue
                if kind == "g1":
                    pe.wait_ge(job_out, JOBS0 + 1)
                    if i >= 2:
                        pe.wait_ge(s_g1l, i - 1)
                    if i == 0:
                        pe.wait_ge(ada_row, 5)
                    mm(PS[:, 4 + i % 2, :], wg2[:, i * P:(i + 1) * P], glow, True, True).then_inc(g1_mm, 1)
                    continue
                n = i
                if n >= 4:
                    pe.wait_ge(job_out, JOBS0 + n - 3)
                out = PS[:, job_bank(n), :]
                if n:
                    piece, ct_ = WIN1 + (n - 1) // 4, (n - 1) % 4
                    landed(pe, piece)
                for kt in range(KT):
                    if n == 0:
                        o_, lhsT, rhs = out[0:16, :], gw[:, kt, :], hT[:, kt, :]
                    elif n < 9:
                        o_, lhsT, rhs = out, piece_ap(piece)[:, kt, ct_ * P:(ct_ + 1) * P], hT[:, kt, :]
                    else:
                        o_, lhsT, rhs = out, hT[:, kt, ct_ * P:(ct_ + 1) * P], piece_ap(piece)[:, kt, :]
                    ins = mm(o_, lhsT, rhs, kt == 0, kt == KT - 1)
                ins.then_inc(job_mm, 1)
                if n and ct_ == 3:
                    used()

            def state_part(t, h, c):
                return ten.matmul(PS[c * CH:(c + 1) * CH, 2 + h, 0:GDV], q1[:, h, t * P + c * CH:t * P + (c + 1) * CH],
                                  state[:, h, :], start=False, stop=True, skip_group_check=True)

            pe.wait_ge(s_kend, GH)
            pe.wait_ge(job_out, JOBS0 + JOBS1)
            def intra(t):
                if t:
                    pe.wait_ge(s_st, 2 * GH * t)
                ts_ = slice(t * P, (t + 1) * P)
                for h in range(GH):
                    ins = mm(PS[:, 0, h * P:(h + 1) * P], k1[:, h, ts_], q1[:, h, ts_], True, True)
                ins.then_inc(it_mm, 1)
                for h in range(GH):
                    ins = ten.transpose(PS[:, 1, h * P:(h + 1) * P], kend[:, h, ts_], ident[:, :])
                ins.then_inc(ke_mm, 1)

            intra(0)
            for t in range(TT):
                if t == 0:
                    pe.wait_ge(s_kz, 1)
                pe.wait_ge(s_ke, t + 1)
                pe.wait_ge(s_it, t + 1)
                if t:
                    pe.wait_ge(s_yt, 2 * t)
                for h in range(GH):
                    for c in range(2):
                        mm(PS[:, (6, 0)[c] + h // 2, (h % 2) * GDV:(h % 2 + 1) * GDV],
                           ketok[c][:, h, :], v1[:, t, h * GDV:(h + 1) * GDV], True, True)
                for h in range(GH):
                    mm(PS[:, 2 + h, 0:GDV], itm[:, h, :], v1[:, t, h * GDV:(h + 1) * GDV], True, True)
                    if t:
                        pe.wait_ge(s_st, 2 * GH * (t - 1) + GH + h + 1)
                    state_part(t, h, 0).then_inc(oi_mm, 1)
                for h in range(GH):
                    pe.wait_ge(s_st, 2 * GH * t + h + 1)
                    state_part(t, h, 1).then_inc(o_mm, 1)
                if t + 1 < TT:
                    intra(t + 1)
                pe.wait_ge(s_yo, t + 1)
                for kt in range(KT):
                    ins = ten.transpose(PS[:, 6 + kt // 4, kt % 4 * P:(kt % 4 + 1) * P], r1[:, t, kt * P:(kt + 1) * P],
                                        ident[:, :])
                    if kt % 4 == 3:
                        ins.then_inc(yt_mm, 1)
            pe.wait_ge(s_yt, 2 * TT)
            output_projection(1, 2, [WOUT1, WOUT1 + 1], lambda kt, t: yT1[:, kt, t * P:(t + 1) * P])
            moe(1, MOE1)


_INS = ['x', 'c', 'router_w', 'router_b', 'ada_w', 'ada_b', 'norm_mix', 'norm_ffn', 'ev_w_in', 'ev_conv_w',
        'ev_conv_b', 'ev_r_w', 'ev_r_b', 'ev_i_w', 'ev_i_b', 'ev_lam', 'ev_forget_b', 'ev_q_gain', 'ev_k_gain',
        'ev_w_out', 'od_w_in', 'od_gate_w2', 'od_gate_b', 'od_out_gain', 'od_w_out', 'moe_w1', 'moe_w3', 'moe_w2']


def kernel(**inputs):
    import numpy as _np
    import concourse.bacc as _bacc
    from concourse import mybir as _mybir
    from concourse.bass_utils import run_bass_kernel_spmd as _run

    nc = _bacc.Bacc("TRN2", target_bir_lowering=False, num_devices=1)
    arrays, args = {}, {}
    for name in _INS:
        a = _np.ascontiguousarray(inputs[name])
        arrays[f"in_{name}"] = a
        args[name] = nc.dram_tensor(f"in_{name}", a.shape, _mybir.dt.from_np(a.dtype), kind="ExternalInput").ap()
    args["out"] = nc.dram_tensor("out_x", (1, T, D), _mybir.dt.float32, kind="ExternalOutput").ap()
    build_program(nc, args)
    r = _run(nc, [arrays], core_ids=[0])
    return r.results[0]["out_x"]
```
